# Optimizing a Trainium2 kernel written in Bass

```python
import math
import jax, jax.numpy as jnp
from jax import lax
import numpy as np

D_MODEL = 1024
BATCH = 1
SEQ = 256
DEPTH = 1
DEC_BATCH = 8
DEC_SEQ = 8
PAST_LEN = 1024
PAGE_SIZE = 128

F32 = jnp.float32
EPS = 1e-6
MIX_WIDTH = D_MODEL // 2
N_BRANCH = 3
SB_HEAD_DIM = 64
SB_HEADS = MIX_WIDTH // SB_HEAD_DIM
SB_WIDTH = SB_HEADS * SB_HEAD_DIM
Q_BLOCK = 128
SSM_HEAD_DIM = 64
SSM_WIDTH = MIX_WIDTH
SSM_HEADS = SSM_WIDTH // SSM_HEAD_DIM
SSM_GROUPS = 2
SSM_STATE = 128
SSM_CONV = 4
SSM_CONV_CH = SSM_WIDTH + 2 * SSM_GROUPS * SSM_STATE
SSM_CHUNK = 128
CF_WIDTH = MIX_WIDTH
CF_CONV = 31
MOE_GROUPS = 4
EXPERTS_PER_GROUP = 4
N_EXPERTS = MOE_GROUPS * EXPERTS_PER_GROUP
TOP_K_IN_GROUP = 2
D_EXPERT = D_MODEL // 2
PLE_DIM = 256
OFF_Q = 0
OFF_K = OFF_Q + SB_WIDTH
OFF_V = OFF_K + SB_WIDTH
OFF_Z = OFF_V + SB_WIDTH
OFF_XBC = OFF_Z + SSM_WIDTH
OFF_DT = OFF_XBC + SSM_CONV_CH
OFF_GLU = OFF_DT + SSM_HEADS
OFF_GATE = OFF_GLU + 2 * CF_WIDTH
IN_COLS = OFF_GATE + N_BRANCH * D_MODEL

kernel_name = 'hybrid_stickbreak_ssd_conformer_hmoe_step'

def rmsnorm(x, g):
    xf = x.astype(F32)
    y = xf * lax.rsqrt(jnp.mean(xf * xf, axis=-1, keepdims=True) + EPS) * g.astype(F32)
    return y.astype(x.dtype)

def layernorm(x, g, b):
    xf = x.astype(F32)
    mu = jnp.mean(xf, axis=-1, keepdims=True)
    xc = xf - mu
    var = jnp.mean(xc * xc, axis=-1, keepdims=True)
    return (xc * lax.rsqrt(var + EPS) * g.astype(F32) + b.astype(F32)).astype(x.dtype)

def causal_dwconv(buf, x, w, b):
    xp = jnp.concatenate([buf.astype(x.dtype), x], axis=1)
    out = lax.conv_general_dilated(xp, w.astype(x.dtype)[:, None, :], window_strides=(1,), padding='VALID',
                                   dimension_numbers=('NWC', 'WIO', 'NWC'), feature_group_count=x.shape[-1])
    return out + b.astype(x.dtype), xp[:, xp.shape[1] - (w.shape[0] - 1):]

def stick_breaking_attention(q, k, v, q_start, sb_bias):
    b, lq, h, dh = q.shape
    lk = k.shape[1]
    qb = Q_BLOCK if lq % Q_BLOCK == 0 else lq
    nb = lq // qb
    scale = dh ** -0.5
    key_pos = jnp.arange(lk)
    q_blocks = q.reshape(b, nb, qb, h, dh).swapaxes(0, 1)
    starts = q_start + jnp.arange(nb) * qb
    bias = sb_bias.astype(F32)[None, :, None, None]

    def block(args):
        qblk, s0 = args
        z = jnp.einsum('bqhd,bkhd->bhqk', qblk, k, preferred_element_type=F32) * scale + bias
        qpos = s0 + jnp.arange(qb)
        mask = key_pos[None, :] < qpos[:, None]
        log_1mb = jnp.where(mask, jax.nn.log_sigmoid(-z), 0.0)
        after = lax.cumsum(log_1mb, axis=3, reverse=True) - log_1mb
        w = jnp.where(mask, jnp.exp(jax.nn.log_sigmoid(z) + after), 0.0)
        return jnp.einsum('bhqk,bkhd->bqhd', w.astype(v.dtype), v)

    out = lax.map(block, (q_blocks, starts))
    return out.swapaxes(0, 1).reshape(b, lq, h, dh)

def ssd_scan(x, dt, a, bm, cm, h0):
    b, L, H, P = x.shape
    G, N = bm.shape[2], bm.shape[3]
    E = H // G
    q = SSM_CHUNK if L % SSM_CHUNK == 0 else L
    nc = L // q

    def chunks(t):
        return t.reshape((b, nc, q) + t.shape[2:]).swapaxes(0, 1)

    xs = chunks(x.astype(F32).reshape(b, L, G, E, P))
    dts = chunks(dt.astype(F32).reshape(b, L, G, E))
    bs = chunks(bm.astype(F32))
    cs = chunks(cm.astype(F32))
    a_ge = a.reshape(G, E)
    causal = jnp.tril(jnp.ones((q, q), dtype=bool))[None, :, :, None, None]

    def step(h, inp):
        xc, dtc, bc, cc = inp
        cum = jnp.cumsum(dtc * a_ge, axis=1)
        seg = cum[:, :, None] - cum[:, None, :]
        decay = jnp.exp(jnp.where(causal, seg, -jnp.inf))
        cb = jnp.einsum('btgn,bsgn->btsg', cc, bc)
        w = cb[..., None] * decay * dtc[:, None]
        y = jnp.einsum('btsge,bsgep->btgep', w, xc)
        y = y + jnp.einsum('btgn,bgepn->btgep', cc, h) * jnp.exp(cum)[..., None]
        w_end = jnp.exp(cum[:, -1:] - cum) * dtc
        h = h * jnp.exp(cum[:, -1])[..., None, None] + jnp.einsum('bsge,bsgep,bsgn->bgepn', w_end, xc, bc)
        return h, y

    h_end, ys = lax.scan(step, h0.astype(F32).reshape(b, G, E, P, N), (xs, dts, bs, cs))
    return ys.swapaxes(0, 1).reshape(b, L, H, P), h_end.reshape(b, H, P, N)

def mamba2_branch(z, xbc, dt_raw, conv_buf, h0, conv_w, conv_b, dt_bias, a_log, d_skip, norm_g):
    b, L, _ = xbc.shape
    xbc_c, conv_new = causal_dwconv(conv_buf, xbc, conv_w, conv_b)
    xbc_c = jax.nn.silu(xbc_c)
    xs = xbc_c[..., :SSM_WIDTH].reshape(b, L, SSM_HEADS, SSM_HEAD_DIM)
    bm = xbc_c[..., SSM_WIDTH:SSM_WIDTH + SSM_GROUPS * SSM_STATE].reshape(b, L, SSM_GROUPS, SSM_STATE)
    cm = xbc_c[..., SSM_WIDTH + SSM_GROUPS * SSM_STATE:].reshape(b, L, SSM_GROUPS, SSM_STATE)
    dt = jax.nn.softplus(dt_raw.astype(F32) + dt_bias.astype(F32))
    a = -jnp.exp(a_log.astype(F32))
    y, h_new = ssd_scan(xs, dt, a, bm, cm, h0)
    y = y + d_skip.astype(F32)[:, None] * xs.astype(F32)
    y = y.reshape(b, L, SSM_WIDTH).astype(z.dtype) * jax.nn.silu(z)
    return rmsnorm(y, norm_g), conv_new, h_new.astype(z.dtype)

def conformer_branch(glu_in, conv_buf, conv_w, conv_b, ln_g, ln_b):
    u = glu_in[..., :CF_WIDTH] * jax.nn.sigmoid(glu_in[..., CF_WIDTH:])
    c, conv_new = causal_dwconv(conv_buf, u, conv_w, conv_b)
    return jax.nn.silu(layernorm(c, ln_g, ln_b)), conv_new

def hier_moe(h, w_rg, b_rg, w_re, b_re, w_gate, w_up, w_down):
    b, L, d = h.shape
    t = h.reshape(-1, d)
    g_logits = (t @ w_rg).astype(F32) + b_rg.astype(F32)
    g_prob = jax.nn.softmax(g_logits, axis=-1)
    g_idx = jnp.argmax(g_logits, axis=-1)
    g_w = jnp.take_along_axis(g_prob, g_idx[:, None], axis=-1)
    e_logits = jnp.einsum('td,dge->tge', t, w_re).astype(F32) + b_re.astype(F32)
    e_sel = jnp.take_along_axis(e_logits, g_idx[:, None, None], axis=1)[:, 0]
    top_v, top_i = lax.top_k(e_sel, TOP_K_IN_GROUP)
    top_w = jax.nn.softmax(top_v, axis=-1) * g_w
    expert_id = g_idx[:, None] * EXPERTS_PER_GROUP + top_i
    combine = jnp.sum(jax.nn.one_hot(expert_id, N_EXPERTS, dtype=F32) * top_w[..., None], axis=1)
    hg = jnp.einsum('td,edf->tef', t, w_gate)
    hu = jnp.einsum('td,edf->tef', t, w_up)
    act = jax.nn.silu(hg) * hu * combine[..., None].astype(t.dtype)
    return jnp.einsum('tef,efd->td', act, w_down).reshape(b, L, d)

def layer_forward(x, p_i, k_past, v_past, ssm_conv_buf, ssm_h0, cf_buf, q_start,
                  norm_mix, w_in, sb_bias, ssm_conv_w, ssm_conv_b, dt_bias, a_log, d_skip, ssm_norm,
                  cf_conv_w, cf_conv_b, cf_ln_g, cf_ln_b, w_branch, w_out,
                  norm_ffn, w_router_group, b_router_group, w_router_expert, b_router_expert,
                  w_expert_gate, w_expert_up, w_expert_down, norm_ple, w_ple_gate, w_ple_proj):
    b, L, _ = x.shape
    h = rmsnorm(x, norm_mix)
    proj = h @ w_in
    q = proj[..., OFF_Q:OFF_K].reshape(b, L, SB_HEADS, SB_HEAD_DIM)
    k_new = proj[..., OFF_K:OFF_V].reshape(b, L, SB_HEADS, SB_HEAD_DIM)
    v_new = proj[..., OFF_V:OFF_Z].reshape(b, L, SB_HEADS, SB_HEAD_DIM)
    if k_past is None:
        k_all, v_all = k_new, v_new
    else:
        k_all = jnp.concatenate([k_past.astype(k_new.dtype), k_new], axis=1)
        v_all = jnp.concatenate([v_past.astype(v_new.dtype), v_new], axis=1)
    a_out = stick_breaking_attention(q, k_all, v_all, q_start, sb_bias).reshape(b, L, SB_WIDTH)
    b_out, ssm_conv_new, ssm_h_new = mamba2_branch(
        proj[..., OFF_Z:OFF_XBC], proj[..., OFF_XBC:OFF_DT], proj[..., OFF_DT:OFF_GLU],
        ssm_conv_buf, ssm_h0, ssm_conv_w, ssm_conv_b, dt_bias, a_log, d_skip, ssm_norm)
    c_out, cf_new = conformer_branch(proj[..., OFF_GLU:OFF_GATE], cf_buf, cf_conv_w, cf_conv_b, cf_ln_g, cf_ln_b)
    branches = jnp.stack([a_out.astype(x.dtype), b_out.astype(x.dtype), c_out.astype(x.dtype)], axis=0)
    u = jnp.einsum('nblw,nwd->nbld', branches, w_branch)
    gates = jax.nn.sigmoid(proj[..., OFF_GATE:].reshape(b, L, N_BRANCH, D_MODEL))
    merged = jnp.einsum('blnd,nbld->bld', gates, u)
    x = x + merged @ w_out
    x = x + hier_moe(rmsnorm(x, norm_ffn), w_router_group, b_router_group, w_router_expert,
                     b_router_expert, w_expert_gate, w_expert_up, w_expert_down)
    ple_gate = jax.nn.sigmoid(rmsnorm(x, norm_ple) @ w_ple_gate)
    x = x + ple_gate * (p_i.astype(x.dtype) @ w_ple_proj)
    return x, k_new, v_new, ssm_h_new, ssm_conv_new, cf_new

def setup_inputs(seed: int = 0) -> dict:
    key = jax.random.key(seed)
    ks = iter(jax.random.split(key, 64))

    def nrm(shape, scale):
        return jax.random.normal(next(ks), shape, F32) * scale

    def gain(shape):
        return 1.0 + nrm(shape, 0.01)

    n_pages = PAST_LEN // PAGE_SIZE
    n_pool = (DEC_BATCH * n_pages * 5) // 4
    x_prompt = nrm((BATCH, SEQ, D_MODEL), 1.0)
    x_sample = nrm((DEC_BATCH, DEC_SEQ, D_MODEL), 1.0)
    p_prompt = nrm((DEPTH, BATCH, SEQ, PLE_DIM), 1.0)
    p_sample = nrm((DEPTH, DEC_BATCH, DEC_SEQ, PLE_DIM), 1.0)
    cache_k = nrm((DEPTH, n_pool, PAGE_SIZE, SB_HEADS, SB_HEAD_DIM), 1.0)
    cache_v = nrm((DEPTH, n_pool, PAGE_SIZE, SB_HEADS, SB_HEAD_DIM), 1.0)
    page_table = jax.random.permutation(next(ks), n_pool)[:DEC_BATCH * n_pages].reshape(DEC_BATCH, n_pages).astype(jnp.int32)
    state_ssm = nrm((DEPTH, DEC_BATCH, SSM_HEADS, SSM_HEAD_DIM, SSM_STATE), 0.1)
    state_ssm_conv = nrm((DEPTH, DEC_BATCH, SSM_CONV - 1, SSM_CONV_CH), 1.0)
    state_cf_conv = nrm((DEPTH, DEC_BATCH, CF_CONV - 1, CF_WIDTH), 0.5)
    sb_bias = jax.random.uniform(next(ks), (DEPTH, SB_HEADS), F32, -7.0, -4.0)
    dt0 = jnp.exp(jax.random.uniform(next(ks), (DEPTH, SSM_HEADS), F32, math.log(1e-3), math.log(1e-1)))
    dt_bias = dt0 + jnp.log(-jnp.expm1(-dt0))
    a_log = jnp.log(jax.random.uniform(next(ks), (DEPTH, SSM_HEADS), F32, 1.0, 16.0))
    return {
        'x_prompt': x_prompt, 'x_sample': x_sample, 'p_prompt': p_prompt, 'p_sample': p_sample,
        'cache_k': cache_k, 'cache_v': cache_v, 'page_table': page_table,
        'state_ssm': state_ssm, 'state_ssm_conv': state_ssm_conv, 'state_cf_conv': state_cf_conv,
        'norm_mix': gain((DEPTH, D_MODEL)),
        'w_in': nrm((DEPTH, D_MODEL, IN_COLS), D_MODEL ** -0.5),
        'sb_bias': sb_bias,
        'ssm_conv_w': nrm((DEPTH, SSM_CONV, SSM_CONV_CH), SSM_CONV ** -0.5),
        'ssm_conv_b': nrm((DEPTH, SSM_CONV_CH), 0.01),
        'dt_bias': dt_bias,
        'a_log': a_log,
        'd_skip': gain((DEPTH, SSM_HEADS)),
        'ssm_norm': gain((DEPTH, SSM_WIDTH)),
        'cf_conv_w': nrm((DEPTH, CF_CONV, CF_WIDTH), CF_CONV ** -0.5),
        'cf_conv_b': nrm((DEPTH, CF_WIDTH), 0.01),
        'cf_ln_g': gain((DEPTH, CF_WIDTH)),
        'cf_ln_b': nrm((DEPTH, CF_WIDTH), 0.01),
        'w_branch': nrm((DEPTH, N_BRANCH, MIX_WIDTH, D_MODEL), MIX_WIDTH ** -0.5),
        'w_out': nrm((DEPTH, D_MODEL, D_MODEL), D_MODEL ** -0.5),
        'norm_ffn': gain((DEPTH, D_MODEL)),
        'w_router_group': nrm((DEPTH, D_MODEL, MOE_GROUPS), D_MODEL ** -0.5),
        'b_router_group': nrm((DEPTH, MOE_GROUPS), 0.01),
        'w_router_expert': nrm((DEPTH, D_MODEL, MOE_GROUPS, EXPERTS_PER_GROUP), D_MODEL ** -0.5),
        'b_router_expert': nrm((DEPTH, MOE_GROUPS, EXPERTS_PER_GROUP), 0.01),
        'w_expert_gate': nrm((DEPTH, N_EXPERTS, D_MODEL, D_EXPERT), D_MODEL ** -0.5),
        'w_expert_up': nrm((DEPTH, N_EXPERTS, D_MODEL, D_EXPERT), D_MODEL ** -0.5),
        'w_expert_down': nrm((DEPTH, N_EXPERTS, D_EXPERT, D_MODEL), D_EXPERT ** -0.5),
        'norm_ple': gain((DEPTH, D_MODEL)),
        'w_ple_gate': nrm((DEPTH, D_MODEL, D_MODEL), D_MODEL ** -0.5),
        'w_ple_proj': nrm((DEPTH, PLE_DIM, D_MODEL), PLE_DIM ** -0.5),
        'norm_final': gain((D_MODEL,)),
    }

def reference(x_prompt, x_sample, p_prompt, p_sample, cache_k, cache_v, page_table,
              state_ssm, state_ssm_conv, state_cf_conv,
              norm_mix, w_in, sb_bias, ssm_conv_w, ssm_conv_b, dt_bias, a_log, d_skip, ssm_norm,
              cf_conv_w, cf_conv_b, cf_ln_g, cf_ln_b, w_branch, w_out,
              norm_ffn, w_router_group, b_router_group, w_router_expert, b_router_expert,
              w_expert_gate, w_expert_up, w_expert_down, norm_ple, w_ple_gate, w_ple_proj, norm_final):
    layer_params = [dict(norm_mix=norm_mix[i], w_in=w_in[i], sb_bias=sb_bias[i],
                         ssm_conv_w=ssm_conv_w[i], ssm_conv_b=ssm_conv_b[i],
                         dt_bias=dt_bias[i], a_log=a_log[i], d_skip=d_skip[i], ssm_norm=ssm_norm[i],
                         cf_conv_w=cf_conv_w[i], cf_conv_b=cf_conv_b[i], cf_ln_g=cf_ln_g[i], cf_ln_b=cf_ln_b[i],
                         w_branch=w_branch[i], w_out=w_out[i], norm_ffn=norm_ffn[i],
                         w_router_group=w_router_group[i], b_router_group=b_router_group[i],
                         w_router_expert=w_router_expert[i], b_router_expert=b_router_expert[i],
                         w_expert_gate=w_expert_gate[i], w_expert_up=w_expert_up[i], w_expert_down=w_expert_down[i],
                         norm_ple=norm_ple[i], w_ple_gate=w_ple_gate[i], w_ple_proj=w_ple_proj[i])
                    for i in range(DEPTH)]

    bp = x_prompt.shape[0]
    xp = x_prompt
    kp, vp, sp, scp, cfp = [], [], [], [], []
    for i in range(DEPTH):
        zeros_ssm_conv = jnp.zeros((bp, SSM_CONV - 1, SSM_CONV_CH), xp.dtype)
        zeros_h = jnp.zeros((bp, SSM_HEADS, SSM_HEAD_DIM, SSM_STATE), F32)
        zeros_cf = jnp.zeros((bp, CF_CONV - 1, CF_WIDTH), xp.dtype)
        xp, k_new, v_new, h_new, sc_new, cf_new = layer_forward(
            xp, p_prompt[i], None, None, zeros_ssm_conv, zeros_h, zeros_cf, 0, **layer_params[i])
        kp.append(k_new); vp.append(v_new); sp.append(h_new); scp.append(sc_new); cfp.append(cf_new)
    y_prompt = rmsnorm(xp, norm_final)

    bs = x_sample.shape[0]
    n_pages = page_table.shape[1]
    past = n_pages * PAGE_SIZE
    xs = x_sample
    ks_, vs_, ss_, scs_, cfs_ = [], [], [], [], []
    for i in range(DEPTH):
        k_past = cache_k[i][page_table].reshape(bs, past, SB_HEADS, SB_HEAD_DIM)
        v_past = cache_v[i][page_table].reshape(bs, past, SB_HEADS, SB_HEAD_DIM)
        xs, k_new, v_new, h_new, sc_new, cf_new = layer_forward(
            xs, p_sample[i], k_past, v_past, state_ssm_conv[i], state_ssm[i], state_cf_conv[i], past,
            **layer_params[i])
        ks_.append(k_new); vs_.append(v_new); ss_.append(h_new); scs_.append(sc_new); cfs_.append(cf_new)
    y_sample = rmsnorm(xs, norm_final)

    return (y_prompt, y_sample,
            jnp.stack(kp), jnp.stack(vp), jnp.stack(sp), jnp.stack(scp), jnp.stack(cfp),
            jnp.stack(ks_), jnp.stack(vs_), jnp.stack(ss_), jnp.stack(scs_), jnp.stack(cfs_))


_drawn_inputs = setup_inputs


def setup_inputs(seed=0):
    import zlib

    import numpy as np

    out = dict(_drawn_inputs(seed))
    spreads = {}
    factors = {'norm_mix': 3.005,
     'ssm_conv_b': 2.999,
     'd_skip': 8.0,
     'ssm_norm': 4.577,
     'cf_conv_b': 3.828,
     'cf_ln_g': 8.0,
     'cf_ln_b': 3.96,
     'norm_ffn': 3.218,
     'b_router_group': 2.834,
     'b_router_expert': 6.936,
     'norm_ple': 8.0,
     'norm_final': 5.382}
    for name, (base, spread) in spreads.items():
        noise = np.random.default_rng([zlib.crc32(name.encode()), seed]).standard_normal(out[name].shape)
        drawn = base * np.exp(spread * noise) if base else spread * noise
        out[name] = __import__('jax').numpy.asarray(drawn.astype(out[name].dtype))
    for name, factor in factors.items():
        out[name] = (out[name] * factor).astype(out[name].dtype)
    return out
```

```python
from contextlib import ExitStack

import concourse.bass as bass
from concourse import mybir

F32 = mybir.dt.float32
I32 = mybir.dt.int32
ALU = mybir.AluOpType
ACT = mybir.ActivationFunctionType
AX = mybir.AxisListType

P = 128


class Chain:

    def __init__(self, eng, sem):
        self.eng, self.sem, self.n, self.i, self.per = eng, sem, 0, None, 0

    def begin(self, i, per):
        self.i, self.per, self.first = i, per, self.n

    def end(self, turns):
        assert self.n - self.first == self.per, (self.n - self.first, self.per)
        self.n += self.per * (turns - 1)
        self.i = None

    def add(self, ins):
        ins.then_inc(self.sem, 1)
        self.n += 1

    def wait(self):
        self.eng.wait_ge(self.sem, self.n if self.i is None else self.i * self.per + self.n)

    def __call__(self, ins):
        self.add(ins)
        self.wait()


def build(nc, a, o):
    _, SEQ, D = a["x_prompt"].shape
    NB, NT, _ = a["x_sample"].shape
    PLE = a["p_prompt"].shape[-1]
    _, POOL, PAGE, H, DH = a["cache_k"].shape
    NPAGE = a["page_table"].shape[1]
    W = H * DH
    _, _, SH, SP_, SN = a["state_ssm"].shape
    KS = a["ssm_conv_w"].shape[1]
    XC = a["ssm_conv_w"].shape[2]
    KC = a["cf_conv_w"].shape[1]
    NE, _, DE = a["w_expert_gate"].shape[1:]
    NG = a["w_router_group"].shape[2]
    EG = NE // NG
    TS = NB * NT
    T = SEQ + TS
    DC, WC, XCC = D // P, W // P, XC // P
    EPS = 1e-6
    BLK = [(0, P), (P, P), (2 * P, TS)]
    assert SEQ == 2 * P and TS == 64 and NB == 8 and NT == 8 and PAGE == P and DH == 64
    assert D == 1024 and W == 512 and XC == 1024 and SN == P and SP_ == 64 and NPAGE == 8
    COL_DT = 4 * W + XC
    COL_GLU = COL_DT + SH
    GROUP = 512
    TQ, TK, TV, TZ, TX, TA, TB = 0, 4, 8, 12, 16, 24, 28

    w_in_v = a["w_in"][0].rearrange("(k p) n -> p k n", p=P)

    with ExitStack() as ctx:
        def sb(name, shape, dt=F32):
            return ctx.enter_context(nc.sbuf_tensor(name, shape, dt))

        def sem(name):
            return ctx.enter_context(nc.semaphore(name))

        ring = sb("ring", [P, 4, 4096])
        proj = sb("proj", [P, 32, T])
        gates = sb("gates", [P, 3 * DC, T])
        x = sb("x", [P, DC, T])
        scratch = sb("scratch", [P, 7696])
        v_tok = sb("v_tok", [P, 3, W])
        att = sb("att", [P, WC, T])
        rows = sb("rows", [P, 3, T])
        reset = sb("reset", [SH, T])
        ident = sb("ident", [P, P])
        ones = sb("ones", [P, P])
        neg_tri = sb("neg_tri", [P, P])
        neg_ones = sb("neg_ones", [P, P])
        row0 = sb("row0", [P, P])
        mask_att = sb("mask_att", [P, 3 * P])
        mask_ssm = sb("mask_ssm", [P, 3 * P])
        mask_ssms = sb("mask_ssms", [TS, TS])
        mask_new = sb("mask_new", [TS, NB, H * NT])
        bias_row = sb("bias_row", [P, NPAGE, H * NT])
        head_of = sb("head_of", [SH, WC, P])
        own_seq = sb("own_seq", [TS, NB])
        eps = sb("eps", [P, 1])
        par_d = sb("par_d", [P, DC, 33])
        par_w = sb("par_w", [P, WC, 4 + KC])
        small = sb("small", [P, 40])
        pages = sb("pages", [1, NB * NPAGE], I32)
        w_router = sb("w_router", [P, DC, NG + NE])

        MIX, FFN, PLN, FIN, CW, CB, CS = 0, 1, 2, 3, 4, 8, 9
        SG, CFB, LNG, LNB, CFW = 0, 1, 2, 3, 4
        sb_bias = small[:, 0:8]
        d_skip = small[:, 8:12]
        router_bias = small[:, 16:16 + NG + NE]
        descend = small[:, 36:36 + EG]
        dt_bias, a_log, e_a = small[0:SH, 12:13], small[0:SH, 13:14], small[0:SH, 14:15]

        h = scratch[:, 0:DC * T].rearrange("p (c t) -> p c t", t=T)
        XPAD, CPAD = SEQ + KS - 1, SEQ + KC - 1
        xw_ = XPAD + NB * (NT + KS - 1)
        cw_ = CPAD + NB * (NT + KC - 1)
        o1 = DC * T
        o2 = o1 + XCC * xw_
        assert o2 + WC * cw_ == 7696
        xpad = scratch[:, o1:o2].rearrange("p (c t) -> p c t", t=xw_)
        cpad = scratch[:, o2:o2 + WC * cw_].rearrange("p (c t) -> p c t", t=cw_)
        xpad_s = [xpad[:, c, XPAD:xw_].rearrange("p (b t) -> p b t", b=NB) for c in range(XCC)]
        cpad_s = [cpad[:, c, CPAD:cw_].rearrange("p (b t) -> p b t", b=NB) for c in range(WC)]

        def slot(s, *shape):
            n = 1
            for d_ in shape:
                n *= d_
            v = ring[:, s, 0:n]
            if len(shape) == 2:
                v = v.rearrange("p (k n) -> p k n", k=shape[0])
            return v

        def loaded(eng, L, i=0, per=0):
            v = 16 * (L // 4 + 1)
            eng.wait_ge(s(f"ring_loaded{L % 4}"), i * (16 * per // 4) + v if per else v)

        x_tok = slot(2, 3, D)
        raw_d = ring[0:33, 3, 0:1024]
        raw_w = ring[0:4 + KC, 3, 1024:1536]
        raw_cf = ring[0:120, 3, 1536:2560].rearrange("p (a c) -> p a c", a=2)
        k_tok = ring[:, 2, 0:3 * W].rearrange("p (b n) -> p b n", b=3)
        xbc_tok = ring[:, 2, 1536:2560]
        u_tok = ring[0:TS, 2, 2560:3584].rearrange("p (g n) -> p g n", g=2)
        states = ring[:, 3, :].rearrange("p (b c n) -> p b c n", b=NB, c=WC)

        def part(off, *shape):
            n = 1
            for d_ in shape:
                n *= d_
            v = scratch[:, off:off + n]
            return v if len(shape) == 1 else v.rearrange("p (k n) -> p k n", k=shape[0])
        xdt, xdec = part(0, 3, W), part(1536, 3, W)
        b_tok = part(3072, 3, 2 * SN)
        cb = part(3840, 2, 3 * P + TS)
        seg = part(4736, 2, 3 * P + TS)
        b_own = part(3840, 4, 2 * SN)[0:TS]
        h0_t = part(5632, 2, 4 * P)
        ecum = part(6656, WC, TS)
        tokp = part(6912, 3, 24)
        prompt_state = part(6984, WC, SN)
        xdt_sq = part(0, WC, T)

        q_head = part(0, H, SEQ)
        q_pair = scratch[:, 2048:2560].rearrange("p (b c k) -> p b c k", b=NB, c=WC)
        k_turn = part(2560, 2, 512)
        soft = part(3584, 2, 512)
        later = part(4608, 2, 512)
        wgt = part(5632, 2, 512)
        w_new = scratch[0:TS, 7168:7680].rearrange("p (b n) -> p b n", b=NB)
        soft_new = rows[:, :, :].rearrange("p a t -> p (a t)")[0:TS, 0:512].rearrange("p (b n) -> p b n", b=NB)
        expert_row = scratch[0:NE, 3072:5120].rearrange("p (e n) -> p e n", e=NE)
        share = gates[:, 0:NE, :]
        share_row = proj[0:NE, 24, :]
        silu_t, act_t = proj[:, 16:20, :], proj[:, 20:24, :]
        merged = proj[:, 0:DC, :]
        p_tok = v_tok[:, :, 0:PLE]
        p_feat = proj[:, 28:28 + PLE // P, :]
        y_tok = slot(0, 3, D)
        R = {}
        off = 2560
        for name, n in (("logit", NG + NE), ("gmax", 1), ("gexp", NG), ("gsum", 1), ("goh", NG), ("gpri", NG),
                        ("gone", 1), ("pick", NE), ("esel", EG), ("m1", 1), ("o1", EG), ("pri", EG), ("one", 1),
                        ("m2", 1), ("o2", EG), ("w1", 1), ("w2", 1), ("den", 1), ("esel2", EG), ("comb4", EG), ("comb", NE)):
            R[name] = scratch[:, off:off + 3 * n].rearrange("p (b n) -> p b n", b=3)
            off += 3 * n
        assert off <= 3072
        w_dt = gates[:, 0, 0:DC * SH].rearrange("p (k n) -> p k n", k=DC)
        head_row = att[0:SH, :, :].rearrange("p c t -> p (c t)")[:, 0:SH * P].rearrange(
            "p (h n) -> p h n", n=P)

        bank = [ctx.enter_context(nc.psum_tensor(f"bank{i}", [P, 512], F32)) for i in range(8)]

        S = {}

        def s(name):
            if name not in S:
                S[name] = sem(name)
            return S[name]

        block = ctx.enter_context(nc.Block())

        @block.sync
        def _(sp):
            sp.dma_start(x_tok[:, 0:2, :], a["x_prompt"][0].rearrange("(b p) d -> p b d", p=P)
                         ).then_inc(s("x_loaded"), 16)
            sp.dma_start(x_tok[0:TS, 2, :], a["x_sample"].rearrange("b t d -> (b t) d")
                         ).then_inc(s("x_loaded"), 16)
            sp.dma_start(w_dt, w_in_v[:, :, COL_DT:COL_GLU]).then_inc(s("w_dt_loaded"), 16)

            def w_group(j, col):
                sp.dma_start(slot(j, DC, GROUP), w_in_v[:, :, col]).then_inc(s(f"w_in_loaded{j}"), 16)

            for j in range(2):
                w_group(j, slice(j * GROUP, (j + 1) * GROUP))
            with sp.Fori(1, COL_DT // GROUP // 2) as i:
                for j in range(2):
                    sp.wait_ge(s("proj_done"), i * 8 + (4 * j - 4))
                    w_group(j, bass.ds((i * 2 + j) * GROUP, GROUP))
            sp.wait_ge(s("par_turned"), 3)
            sp.dma_start(states, a["state_ssm"][0].rearrange("b (c e) p n -> (e p) b c n", e=2)
                         ).then_inc(s("states_loaded"), 16)
            with sp.Fori(0, (2 * W + 3 * D) // GROUP // 2) as i:
                for j in range(2):
                    sp.wait_ge(s("proj_done"), i * 8 + (20 + 4 * j))
                    w_group(j, bass.ds((i * 2 + j) * GROUP + COL_GLU, GROUP))

            sp.wait_ge(s("pages_loaded"), 16)

            def sequence(u, b):
                for which, cache in (("k", a["cache_k"]), ("v", a["cache_v"])):
                    dst = slot((2, 0)[u] + (which == "v"), NPAGE, W)
                    if which == "k":
                        regs = [sp.value_load(pages[0:1, bass.ds(b * NPAGE + p, 1)], min_val=0, max_val=POOL - 1)
                                for p in range(NPAGE)]
                    for p in range(NPAGE):
                        sp.dma_start(dst[:, p, :],
                                     cache[0][bass.ds(regs[p], 1)].rearrange("n s h d -> (n s) (h d)")
                                     ).then_inc(s(f"{which}_loaded{u}"), 16)

            sp.wait_ge(s("slot2_stored"), 1)
            sp.wait_ge(s("slot3_stored"), 1)
            sequence(0, 0)
            sp.wait_ge(s("proj_done"), 56)
            sequence(1, 1)
            with sp.Fori(1, NB // 2) as i:
                for u in range(2):
                    sp.wait_ge(s("k_page_turned"), i * 16 + (8 * u - 8))
                    sp.wait_ge(s("o_done"), i * 2 + (u - 1))
                    sequence(u, i * 2 + u)

            def ring_load(L, dst, src):
                sp.dma_start(dst, src).then_inc(s(f"ring_loaded{L % 4}"), 16)

            def halves(w, j):
                return w[0].rearrange("(k p) n -> p k n", p=P)[:, :, j * GROUP:(j + 1) * GROUP]

            def expert(L, e, r, turns_free):
                w, k, n = (("w_expert_gate", DC, DE), ("w_expert_up", DC, DE), ("w_expert_down", DE // P, D))[r]
                sem_, v = turns_free
                sp.wait_ge(s(sem_), v)
                ring_load(L, slot(L % 4, k, n), a[w][0][bass.ds(e, 1)].rearrange("e (k p) n -> p (e k) n", p=P))

            def before(e, r):
                return (("down_done", e * DC + (-DC)), ("gate_done", e * 4), ("up_done", e * 4))[r]

            sp.wait_ge(s("k_page_turned"), 8 * NB)
            sp.wait_ge(s("o_done"), NB)
            for L, n in enumerate((1, 2, 0)):
                ring_load(L, slot(L % 4, WC, D), a["w_branch"][0, n].rearrange("(k p) n -> p k n", p=P))
            ring_load(3, slot(3, DC, GROUP), halves(a["w_out"], 0))
            sp.wait_ge(s("branch_done"), DC)
            ring_load(4, slot(0, DC, GROUP), halves(a["w_out"], 1))
            sp.wait_ge(s("po_done"), H)
            sp.dma_start(p_tok[:, 0:2, :], a["p_prompt"][0, 0].rearrange("(b p) n -> p b n", p=P)).then_inc(s("p_loaded"), 16)
            sp.dma_start(p_tok[0:TS, 2, :], a["p_sample"][0].rearrange("b t n -> (b t) n")).then_inc(s("p_loaded"), 16)
            first = [("branch_done", 2 * DC), ("branch_done", 3 * DC), ("out_done", 4), ("out_done", DC)]
            for n in range(12):
                expert(5 + n, n // 3, n % 3, first[n] if n < 4 else before(n // 3, n % 3))
            with sp.Fori(1, NE // 4) as i:
                for n in range(12):
                    e = i * 4 + n // 3
                    sem_, per, base = (("down_done", 4 * DC, (n // 3 - 1) * DC), ("gate_done", 16, n // 3 * 4),
                                       ("up_done", 16, n // 3 * 4))[n % 3]
                    expert(5 + n, e, n % 3, (sem_, i * per + base))
            L = 5 + 3 * NE
            sp.wait_ge(s("down_done"), DC * (NE - 1))
            ring_load(L, slot(L % 4, DC, GROUP), halves(a["w_ple_gate"], 0))
            sp.wait_ge(s("gate_done"), 4 * NE)
            ring_load(L + 1, slot((L + 1) % 4, DC, GROUP), halves(a["w_ple_gate"], 1))
            sp.wait_ge(s("up_done"), 4 * NE)
            ring_load(L + 2, slot((L + 2) % 4, PLE // P, D), a["w_ple_proj"][0].rearrange("(k p) n -> p k n", p=P))

        @block.gpsimd
        def _(pool):
            ch = Chain(pool, s("pool_chain"))

            def where(t, pattern, base, cm, op, fill):
                return pool.affine_select(out=t, in_=t, compare_op=op, fill=fill, base=base,
                                          pattern=pattern, channel_multiplier=cm)

            pool.memset(eps[:, :], EPS).then_inc(s("const"), 1)
            ch(pool.memset(ident[:, :], 0.0))
            where(ident[:, :], [[-1, P]], 0, 1, ALU.not_equal, 1.0).then_inc(s("ident_ready"), 1)
            pool.memset(ones[:, :], 1.0).then_inc(s("const"), 1)
            pool.memset(xpad[:, :, 0:KS - 1], 0.0).then_inc(s("const"), 1)
            pool.memset(cpad[:, :, 0:KC - 1], 0.0).then_inc(s("const"), 1)
            ch.add(pool.memset(neg_ones[:, :], -1.0))
            ch.add(pool.memset(neg_tri[:, :], -1.0))
            ch.add(pool.memset(row0[:, :], 1.0))
            ch.add(pool.memset(mask_att[:, :], 1.0))
            ch.add(pool.memset(mask_ssm[:, :], 1.0))
            ch.add(pool.memset(mask_ssms[:, :], 1.0))
            ch.add(pool.memset(mask_new[:, :, :], 1.0))
            ch.add(pool.memset(reset[:, :], 1.0))
            for j in range(EG):
                ch.add(pool.memset(descend[:, j:j + 1], float(EG - j)))
            ch.add(pool.memset(bias_row[:, :, :], 0.0))
            ch.add(pool.memset(head_row, 0.0))
            ch.add(pool.memset(head_of[:, :, :], 0.0))
            ch(pool.memset(own_seq[:, :], 1.0))
            n = 0
            for ins in [
                where(neg_tri[:, :], [[-1, P]], 0, 1, ALU.is_ge, 0.0),
                where(row0[:, :], [[0, P]], 0, -1, ALU.is_ge, 0.0),
                where(mask_att[:, 0:P], [[1, P]], -1, -1, ALU.is_ge, 0.0),
                where(mask_att[:, 2 * P:3 * P], [[1, P]], -1, -1, ALU.is_ge, 0.0),
                where(mask_ssm[:, 0:P], [[1, P]], 0, -1, ALU.is_ge, 0.0),
                where(mask_ssm[:, 2 * P:3 * P], [[1, P]], 0, -1, ALU.is_ge, 0.0),
                where(head_row, [[-1, SH], [0, P]], 0, 1, ALU.not_equal, 1.0),
                where(head_of[:, :, :].rearrange("h c (e p) -> h c e p", e=2),
                      [[-2, WC], [-1, 2], [0, DH]], 0, 1, ALU.not_equal, 1.0),
            ]:
                ch.add(ins)
            m4 = mask_new[:, :, :].rearrange("s b (h t) -> s b h t", h=H)
            seq_s = mask_ssms[:, :].rearrange("s (b t) -> s b t", b=NB)
            ch.add(where(m4, [[-NT, NB], [0, H], [0, NT]], 0, 1, ALU.is_ge, 0.0))
            ch.add(where(seq_s, [[-NT, NB], [0, NT]], 0, 1, ALU.is_ge, 0.0))
            ch.add(where(own_seq[:, :], [[-NT, NB]], 0, 1, ALU.is_ge, 0.0))
            ch.add(where(reset[:, 0:1], [[0, 1]], 0, 0, ALU.not_equal, 0.0))
            ch(where(reset[:, SEQ:T].rearrange("h (b t) -> h b t", b=NB), [[0, NB], [1, NT]], 0, 0,
                     ALU.not_equal, 0.0))
            ch.add(where(m4, [[NT, NB], [0, H], [1, NT]], -1, -1, ALU.is_ge, 0.0))
            ch.add(where(seq_s, [[NT, NB], [1, NT]], 0, -1, ALU.is_ge, 0.0))
            ch(where(own_seq[:, :], [[NT, NB]], NT - 1, -1, ALU.is_ge, 0.0))
            pool.sem_inc(s("masks"), 1)

            def store(dst, src):
                store.n += 1
                pool.dma_start(dst, src).then_inc(s("stored"), 16)
            store.n = 0

            def store_tokens(prompt, sample, tok):
                store(prompt.rearrange("(b p) n -> p b n", p=P), tok[:, 0:2, :])
                store(sample, tok[0:TS, 2, :])

            pool.wait_ge(s("k_tok_ready"), 3)
            store_tokens(o["k_prompt"][0, 0].rearrange("t h d -> t (h d)"),
                         o["k_sample"][0].rearrange("b t h d -> (b t) (h d)"), k_tok)
            pool.wait_ge(s("v_tok_ready"), 3)
            store_tokens(o["v_prompt"][0, 0].rearrange("t h d -> t (h d)"),
                         o["v_sample"][0].rearrange("b t h d -> (b t) (h d)"), v_tok)
            pool.wait_ge(s("xbc_tok_ready"), 2)
            store(o["ssm_conv_prompt"][0, 0], xbc_tok[P - TS - (KS - 1):P - TS, :])
            for b in range(NB):
                store(o["ssm_conv_sample"][0, b], xbc_tok[P - TS + NT * (b + 1) - (KS - 1):P - TS + NT * (b + 1), :])
            keep = KC - 1 - NT
            store(o["cf_conv_sample"][0][:, 0:keep, :], a["state_cf_conv"][0][:, NT:KC - 1, :])
            pool.wait_ge(s("u_tok_ready"), 2)
            store(o["cf_conv_prompt"][0, 0], u_tok[TS - (KC - 1):TS, 0, :])
            for b in range(NB):
                store(o["cf_conv_sample"][0, b, keep:KC - 1, :], u_tok[NT * b:NT * (b + 1), 1, :])
            pool.wait_ge(s("stored"), 16 * store.n)
            pool.sem_inc(s("slot2_stored"), 1)
            pool.wait_ge(s("prompt_state_ready"), 1)
            store(o["ssm_prompt"][0, 0].rearrange("(c e) p n -> (e p) c n", e=2), prompt_state)
            pool.wait_ge(s("states_new"), 2)
            store(o["ssm_sample"][0].rearrange("b (c e) p n -> (e p) b c n", e=2), states)
            pool.wait_ge(s("stored"), 16 * store.n)
            pool.sem_inc(s("slot3_stored"), 1)

            pool.wait_ge(s("po_done"), H)
            ch(pool.memset(expert_row, 0.0))
            where(expert_row, [[-1, NE], [0, P]], 0, 1, ALU.not_equal, 1.0).then_inc(s("expert_row_ready"), 1)
            for i_, (t0, n) in enumerate(BLK):
                pool.wait_ge(s("y_low_ready"), i_ + 1)
                pool.wait_ge(s("y_high_ready"), i_ + 1)
                store(o["y_prompt"][0, t0:t0 + n, :] if i_ < 2 else o["y_sample"].rearrange("b t d -> (b t) d"),
                      y_tok[0:n, i_, :])
            pool.wait_ge(s("stored"), 16 * store.n)

        @block.scalar
        def _(act):
            ch = Chain(act, s("act_chain"))
            F = act.activation
            for r, name in ((MIX, "norm_mix"), (FFN, "norm_ffn"), (PLN, "norm_ple")):
                act.dma_start(raw_d[r:r + 1, :], a[name]).then_inc(s("par_loaded"), 16)
            act.dma_start(raw_d[FIN:FIN + 1, :], a["norm_final"].unsqueeze(0)).then_inc(s("par_loaded"), 16)
            act.dma_start(raw_d[CW:CW + KS, :], a["ssm_conv_w"][0]).then_inc(s("par_loaded"), 16)
            act.dma_start(raw_d[CB:CB + 1, :], a["ssm_conv_b"]).then_inc(s("par_loaded"), 16)
            act.dma_start(raw_d[CS:33, :], a["state_ssm_conv"][0].rearrange("b t c -> (b t) c")).then_inc(s("par_loaded"), 16)
            for r, name in ((SG, "ssm_norm"), (CFB, "cf_conv_b"), (LNG, "cf_ln_g"), (LNB, "cf_ln_b")):
                act.dma_start(raw_w[r:r + 1, :], a[name]).then_inc(s("par_loaded"), 16)
            act.dma_start(raw_w[CFW:CFW + KC, :], a["cf_conv_w"][0]).then_inc(s("par_loaded"), 16)
            act.dma_start(raw_cf, a["state_cf_conv"][0].rearrange("(a b) t c -> (b t) a c", a=2)).then_inc(s("par_loaded"), 16)
            act.dma_start(sb_bias, a["sb_bias"][0].unsqueeze(0).broadcast_to((P, H))).then_inc(s("small_loaded"), 16)
            for e in range(2):
                act.dma_start(d_skip[e * DH:(e + 1) * DH, :],
                              a["d_skip"][0].rearrange("(c e) -> e c", e=2)[e:e + 1, :].broadcast_to((DH, WC)),
                              allow_slow_non_contiguous=True).then_inc(s("small_loaded"), 16)
            act.dma_start(dt_bias, a["dt_bias"][0].unsqueeze(1)).then_inc(s("small_loaded"), 16)
            act.dma_start(a_log, a["a_log"][0].unsqueeze(1)).then_inc(s("small_loaded"), 16)
            act.dma_start(w_router[:, :, 0:NG], a["w_router_group"][0].rearrange("(k p) g -> p k g", p=P)).then_inc(s("small_loaded"), 16)
            act.dma_start(w_router[:, :, NG:NG + NE], a["w_router_expert"][0].rearrange("(k p) g e -> p k (g e)", p=P)).then_inc(s("small_loaded"), 16)

            act.dma_start(router_bias[:, 0:NG], a["b_router_group"].broadcast_to((P, NG))).then_inc(s("small_loaded"), 16)
            act.dma_start(router_bias[:, NG:NG + NE], a["b_router_expert"].rearrange("a g e -> a (g e)").broadcast_to((P, NE))
                          ).then_inc(s("small_loaded"), 16)
            act.dma_start(pages[:, :], a["page_table"].rearrange("(o b) p -> o (b p)", o=1)).then_inc(s("pages_loaded"), 16)

            def copy(out, in_):
                return F(out, in_, ACT.Copy)

            for c in range(DC):
                act.wait_ge(s("x_turned"), c + 1)
                copy(x[:, c, :], bank[c % 4][:, 0:T]).then_inc(s("x_ready"), 1)

            def norm_square(k):
                F(h[:, 0:DC // 2, :], x[:, 0:DC // 2, :], ACT.Square).then_inc(s("norm_squared"), 1)

            def norm_root(k, width):
                act.wait_ge(s("norm_summed"), k + 1)
                F(rows[:, 0, :], bank[7][:, 0:T], ACT.Sqrt, bias=eps[:, 0:1], scale=1.0 / width
                  ).then_inc(s("norm_rooted"), 1)

            act.wait_ge(s("x_ready"), DC)
            act.wait_ge(s("const"), 1)
            norm_square(0)
            norm_root(0, D)

            act.wait_ge(s("par_turned"), 3)
            copy(par_d[:, :, :], bank[4][:, 0:DC * 33].rearrange("p (c n) -> p c n", c=DC)).then_inc(s("par_ready"), 1)
            copy(par_w[:, :, :], bank[5][:, 0:WC * (4 + KC)].rearrange("p (c n) -> p c n", c=WC)).then_inc(s("par_ready"), 1)
            for c in range(WC):
                src = bank[6 - 2 * (c // 2)][:, 256 * (c % 2):256 * (c % 2) + 240] if c < 2 else \
                    bank[3][:, 256 * (c % 2):256 * (c % 2) + 240]
                copy(cpad_s[c][:, :, 0:KC - 1], src.rearrange("p (b t) -> p b t", b=NB)).then_inc(s("par_ready"), 1)

            act.sem_inc(s("proj_evac"), 4)
            with act.Fori(0, 4) as i:
                for t in range(8):
                    act.wait_ge(s("proj_done"), i * 8 + (t + 1))
                    copy(proj[:, bass.ds(i * 8 + t, 1), :].rearrange("p c t -> p (c t)"), bank[t % 4][:, 0:T]
                         ).then_inc(s("proj_evac"), 1)
            act.wait_ge(s("proj_evac"), 36)
            F(proj[:, TB:TB + WC, :], proj[:, TB:TB + WC, :], ACT.Sigmoid).then_inc(s("glu_sigmoid"), 1)

            def turned(name, out, b):
                act.wait_ge(s(name + "_turned"), turned.n.setdefault(name, 0) + 1)
                turned.n[name] += 1
                copy(out, b).then_inc(s(name + "_tok_ready"), 1)
            turned.n = {}
            for name, tok in (("k", k_tok), ("v", v_tok)):
                for i_, (t0, n) in enumerate(BLK):
                    turned(name, tok[0:n, i_, :], bank[5 + (i_ + (name == "v")) % 2][0:n, :])
            for i_ in range(2):
                turned("xbc", xbc_tok[:, 512 * i_:512 * (i_ + 1)], bank[5 + i_ % 2][:, :])

            with act.Fori(0, 3) as i:
                for t in range(8):
                    act.wait_ge(s("proj_done"), i * 8 + (32 + t + 1))
                    F(gates[:, bass.ds(i * 8 + t, 1), :].rearrange("p c t -> p (c t)"), bank[t % 4][:, 0:T],
                      ACT.Sigmoid).then_inc(s("proj_evac"), 1)

            act.wait_ge(s("u_turned"), 1)
            for g in range(2):
                copy(u_tok[:, g, :], bank[5 + g][0:TS, :]).then_inc(s("u_tok_ready"), 1)
            norm_root(1, W)
            for c in range(WC):
                act.wait_ge(s("ln_scaled"), 1)
                F(proj[:, TA + c, :], proj[:, TA + c, :], ACT.Silu, bias=par_w[:, c, LNB:LNB + 1],
                  scale=par_w[:, c, LNG:LNG + 1]).then_inc(s("cf_ready"), 1)
            act.wait_ge(s("xconv_done"), 1)
            F(proj[:, TX:TX + XCC, :], proj[:, TX:TX + XCC, :], ACT.Silu).then_inc(s("xconv_silu"), 1)
            F(proj[:, TZ:TZ + WC, :], proj[:, TZ:TZ + WC, :], ACT.Silu).then_inc(s("z_silu"), 1)
            act.wait_ge(s("cf_ready"), WC)
            act.wait_ge(s("small_loaded"), 16 * 9)
            act.wait_ge(s("dt_done"), 1)
            F(rows[0:SH, 0, :], bank[4][0:SH, 0:T], ACT.Identity, bias=dt_bias).then_inc(s("dt_raw"), 1)
            act.wait_ge(s("dt_raw"), 1)
            ch(F(rows[0:SH, 1, :], rows[0:SH, 0, :], ACT.Abs))
            ch(F(rows[0:SH, 1, :], rows[0:SH, 1, :], ACT.Exp, scale=-1.0))
            F(e_a, a_log, ACT.Exp).then_inc(s("dt_log"), 1)
            F(rows[0:SH, 1, :], rows[0:SH, 1, :], ACT.Ln, bias=1.0).then_inc(s("dt_log"), 1)
            act.wait_ge(s("decay_arg"), 2)
            F(rows[0:SH, 1, :], rows[0:SH, 1, :], ACT.Exp).then_inc(s("decay_exp"), 1)
            F(reset[:, 0:TS], rows[0:SH, 2, SEQ:T], ACT.Exp).then_inc(s("ecum_ready"), 1)
            for i_, (t0, n) in enumerate(BLK):
                act.wait_ge(s("b_turned"), max(i_ + 1, 2))
                copy(b_tok[0:n, i_, :], bank[3 + 3 * (i_ // 2)][0:n, 256 * (i_ % 2):256 * (i_ % 2) + 256]
                     ).then_inc(s("b_tok_ready"), 1)
            for hd in range(SH):
                act.wait_ge(s("seg_ready"), 3 * (hd + 1))
                F(seg[:, hd % 2, 0:3 * P], seg[:, hd % 2, 0:3 * P], ACT.Exp).then_inc(s("seg_exp"), 1)
                F(seg[0:TS, hd % 2, 3 * P:3 * P + TS], seg[0:TS, hd % 2, 3 * P:3 * P + TS], ACT.Exp
                  ).then_inc(s("seg_exp"), 1)
                act.wait_ge(s("y_done"), hd + 1)
                e = hd % 2
                copy(proj[e * DH:(e + 1) * DH, TB + hd // 2, :], bank[2 + hd % 2][e * DH:(e + 1) * DH, 0:T]
                     ).then_inc(s("y_ready"), 1)
            for b in range(NB):
                act.wait_ge(s("h0_turned"), b + 1)
                if b >= 2:
                    act.wait_ge(s("y_state_done"), b - 1)
                copy(h0_t[:, b % 2, :], bank[6 + b % 2][:, :]).then_inc(s("h0_ready"), 1)
            act.wait_ge(s("prompt_state_done"), 1)
            copy(prompt_state.rearrange("p c n -> p (c n)"), bank[5][:, :]).then_inc(s("prompt_state_ready"), 1)
            norm_root(2, W)

            def softplus_log(out, z, n, **bias):
                ch(F(out, z, ACT.Abs, **bias))
                ch(F(out, out, ACT.Exp, scale=-1.0))
                return F(out, out, ACT.Ln, bias=1.0)

            act.wait_ge(s("zn_done"), 1)
            act.wait_ge(s("slot3_stored"), 1)
            softplus_log(w_new, bank[4][0:TS, :].rearrange("p (b n) -> p b n", b=NB), TS).then_inc(s("zn_log"), 1)
            act.wait_ge(s("wn_arg"), 1)
            F(w_new, w_new, ACT.Exp).then_inc(s("wn_exp"), 1)
            act.sem_inc(s("even_copied"), 1)
            with act.Fori(0, NB // 2) as i:
                ch.begin(i, 4)
                for u in range(2):
                    for p in range(0, NPAGE, 2):
                        act.wait_ge(s("k_page_turned"), i * 16 + (8 * u + p + 1))
                        copy(k_turn[:, 0, :], bank[0][:, :]).then_inc(s("even_copied"), 1)
                    act.wait_ge(s("z_done"), i * 2 + (u + 1))
                    softplus_log(wgt[:, u, :], bank[2 + u][:, :], P).then_inc(s("z_log"), 1)
                for u in range(2):
                    act.wait_ge(s("c_done"), i * 2 + (u + 1))
                    F(wgt[:, u, :], bank[2 + u][:, :], ACT.Exp).then_inc(s("wgt_ready"), 1)
                ch.end(NB // 2)
            for hd in range(H):
                u, e, b_h = hd % 2, hd % 2, sb_bias[:, hd:hd + 1]
                act.wait_ge(s("pz_done"), hd + 1)
                softplus_log(wgt[:, u, 0:3 * P], bank[u][:, 0:3 * P], P, bias=b_h).then_inc(s("pz_log"), 1)
                act.wait_ge(s("pw_arg"), hd + 1)
                F(wgt[:, u, 0:3 * P], wgt[:, u, 0:3 * P], ACT.Exp).then_inc(s("pw_exp"), 1)
                act.wait_ge(s("po_done"), hd + 1)
                copy(att[e * DH:(e + 1) * DH, hd // 2, 0:SEQ], bank[2 + u][e * DH:(e + 1) * DH, 0:SEQ]
                     ).then_inc(s("att_ready"), 1)

            act.wait_ge(s("out_added"), DC)
            norm_square(3)
            norm_root(3, D)
            act.wait_ge(s("g_arg"), 1)
            F(R["gexp"], R["gexp"], ACT.Exp).then_inc(s("g_exp"), 1)
            act.wait_ge(s("e_arg"), 1)
            F(R["w2"], R["w2"], ACT.Exp).then_inc(s("e_exp"), 1)
            act.wait_ge(s("comb_turned"), 1)
            copy(share_row, bank[3][0:NE, 0:T]).then_inc(s("share_row_ready"), 1)
            for e in range(NE):
                act.wait_ge(s("share_spread"), e + 1)
                copy(share[:, e, :], bank[4 + e % 4][:, 0:T]).then_inc(s("share_ready"), 1)
            with act.Fori(0, NE // 4) as i:
                for t in range(16):
                    act.wait_ge(s("gate_done"), i * 16 + (t + 1))
                    F(silu_t[:, t % 4, :], bank[t % 4][:, 0:T], ACT.Silu).then_inc(s("silu_ready"), 1)

            act.wait_ge(s("down_added"), 8 + DC * NE)
            norm_square(4)
            norm_root(4, D)
            act.wait_ge(s("p_turned"), 1)
            for c in range(PLE // P):
                copy(p_feat[:, c, :], bank[4 + c][:, 0:T]).then_inc(s("p_ready"), 1)
            for m in range(DC):
                act.wait_ge(s("pg_done"), m + 1)
                if m >= 4:
                    act.wait_ge(s("pple_added"), m - 3)
                F(silu_t[:, m % 4, :], bank[m % 4][:, 0:T], ACT.Sigmoid).then_inc(s("pg_ready"), 1)
            act.wait_ge(s("pple_added"), DC)
            norm_square(5)
            norm_root(5, D)
            for i_, (t0, n) in enumerate(BLK):
                act.wait_ge(s("y_turned"), 2 * i_ + 1)
                copy(y_tok[0:n, i_, 0:512], bank[2 * i_][0:n, :]).then_inc(s("y_low_ready"), 1)

        @block.vector
        def _(dve):
            ch = Chain(dve, s("dve_chain"))
            TT, TSC, STT = dve.tensor_tensor, dve.tensor_scalar, dve.scalar_tensor_tensor

            def norm_square(k):
                TT(h[:, DC // 2:DC, :], x[:, DC // 2:DC, :], x[:, DC // 2:DC, :], ALU.mult
                   ).then_inc(s("norm_squared"), 1)

            def norm_inverse(k, width):
                r, v, t = rows[:, 0, :], rows[:, 1, :], rows[:, 2, :]
                dve.wait_ge(s("norm_rooted"), k + 1)
                ch.add(TSC(v, bank[7][:, 0:T], 1.0 / width, EPS, ALU.mult, ALU.add))
                ch(dve.reciprocal(r, r))
                ch(TT(t, r, r, ALU.mult))
                ch(TT(t, t, v, ALU.mult))
                ch(TSC(t, t, -0.5, 1.5, ALU.mult, ALU.add))
                ch(TT(r, r, t, ALU.mult))

            def norm_apply(col):
                for c in range(DC):
                    STT(h[:, c, :], x[:, c, :], par_d[:, c, col:col + 1], rows[:, 0, :], ALU.mult, ALU.mult
                        ).then_inc(s("h_ready"), 1)

            dve.wait_ge(s("x_ready"), DC)
            norm_square(0)
            norm_inverse(0, D)
            dve.wait_ge(s("par_ready"), 1)
            norm_apply(MIX)

            dve.wait_ge(s("proj_evac"), 4 + 24)
            dve.wait_ge(s("const"), 4)
            dve.wait_ge(s("par_ready"), 2 + WC)
            ch.add(TSC(proj[:, TQ:TQ + WC, :], proj[:, TQ:TQ + WC, :], float(DH) ** -0.5, None, ALU.mult))
            ch.add(dve.tensor_copy(xpad[:, :, KS - 1:XPAD], proj[:, TX:TX + XCC, 0:SEQ]))
            for c in range(XCC):
                ch.add(dve.tensor_copy(xpad_s[c][:, :, 0:KS - 1],
                                       par_d[:, c, CS:33].rearrange("p (b t) -> p b t", b=NB)))
                ch.add(dve.tensor_copy(xpad_s[c][:, :, KS - 1:],
                                       proj[:, TX + c, SEQ:T].rearrange("p (b t) -> p b t", b=NB)))
            ch.wait()
            dve.wait_ge(s("glu_sigmoid"), 1)
            TT(cpad[:, :, KC - 1:CPAD], proj[:, TA:TA + WC, 0:SEQ], proj[:, TB:TB + WC, 0:SEQ], ALU.mult
               ).then_inc(s("u_ready"), 1)
            ch(TT(proj[:, TB:TB + WC, SEQ:T], proj[:, TA:TA + WC, SEQ:T], proj[:, TB:TB + WC, SEQ:T], ALU.mult))
            for c in range(WC):
                dve.tensor_copy(cpad_s[c][:, :, KC - 1:], proj[:, TB + c, SEQ:T].rearrange("p (b t) -> p b t", b=NB)
                                ).then_inc(s("u_ready"), 1)
            dve.wait_ge(s("u_ready"), 1 + WC)

            def conv(tile, pad, pads, K, n, par, w0, bias):
                for k in range(K):
                    for c in range(n):
                        for out, src in ((proj[:, tile + c, 0:SEQ], pad[:, c, k:k + SEQ]),
                                         (proj[:, tile + c, SEQ:T].rearrange("p (b t) -> p b t", b=NB),
                                          pads[c][:, :, k:k + NT])):
                            w = par[:, c, w0 + k:w0 + k + 1]
                            if k == 0:
                                ch.add(TSC(out, src, w, par[:, c, bias:bias + 1], ALU.mult, ALU.add))
                            else:
                                ch.add(STT(out, src, w, out, ALU.mult, ALU.add))
                    ch.wait()

            conv(TA, cpad, cpad_s, KC, WC, par_w, CFW, CFB)
            dve.sem_inc(s("cconv_done"), 1)
            dve.wait_ge(s("xbc_turned"), 2)
            conv(TX, xpad, xpad_s, KS, XCC, par_d, CW, CB)
            dve.sem_inc(s("xconv_done"), 1)

            cf = proj[:, TA:TA + WC, :]
            dve.wait_ge(s("mean_summed"), 1)
            ch(TSC(rows[:, 1, :], bank[6][:, 0:T], 1.0 / W, None, ALU.mult))
            ch(TT(cf, cf, rows[:, 1:2, :].broadcast_to((P, WC, T)), ALU.subtract))
            dve.wait_ge(s("proj_done"), 56)
            TT(h[:, 0:WC, :], cf, cf, ALU.mult).then_inc(s("norm_squared"), 1)
            norm_inverse(1, W)
            TT(cf, cf, rows[:, 0:1, :].broadcast_to((P, WC, T)), ALU.mult).then_inc(s("ln_scaled"), 1)

            dve.wait_ge(s("masks"), 1)
            dve.wait_ge(s("small_loaded"), 16 * 9)
            dve.tensor_copy(bias_row[0:1, :, :].rearrange("p a (h t) -> p a h t", h=H),
                            sb_bias[0:1, :].unsqueeze(1).unsqueeze(3).broadcast_to((1, NPAGE, H, NT))
                            ).then_inc(s("bias_row_ready"), 1)

            dt, dec, cum = (rows[0:SH, j, :] for j in range(3))
            dve.wait_ge(s("dt_raw"), 1)
            dve.wait_ge(s("dt_log"), 2)
            dve.wait_ge(s("masks"), 1)
            ch(STT(dt, dt, 0.0, dec, ALU.max, ALU.add))
            ch(TSC(dec, dt, e_a, -1.0, ALU.mult, ALU.mult))
            ch(dve.tensor_tensor_scan(cum, reset[:, :], dec, 0.0, ALU.mult, ALU.add))
            TSC(dec[:, 0:SEQ], cum[:, 0:SEQ], -1.0, cum[:, SEQ - 1:SEQ], ALU.mult, ALU.add
                ).then_inc(s("decay_arg"), 1)
            cum_s = cum[:, SEQ:T].rearrange("h (b t) -> h b t", b=NB)
            TT(dec[:, SEQ:T].rearrange("h (b t) -> h b t", b=NB), cum_s[:, :, NT - 1:NT].broadcast_to((SH, NB, NT)), cum_s,
               ALU.subtract).then_inc(s("decay_arg"), 1)
            dve.wait_ge(s("decay_exp"), 1)
            TT(dec, dec, dt, ALU.mult).then_inc(s("rows_ready"), 1)
            dve.wait_ge(s("rows_turned"), 1)
            for i_, (n, b0, nb) in enumerate(((P, 0, 2), (TS, 2, 1))):
                src = bank[5][0:n, 24 * b0:24 * (b0 + nb)].rearrange("p (b k) -> p b k", b=nb)
                ch.add(dve.tensor_copy(tokp[0:n, b0:b0 + nb, 0:16], src[:, :, 0:16]))
                ch.add(TSC(tokp[0:n, b0:b0 + nb, 16:24], src[:, :, 16:24], -1.0, None, ALU.mult))
            ch.wait()
            dve.sem_inc(s("tokp_ready"), 1)
            for i_, (t0, n) in enumerate(BLK):
                dve.wait_ge(s("xs_turned"), i_ + 1)
                for j, out in enumerate((xdt, xdec)):
                    TT(out[0:n, i_, :].rearrange("p (h d) -> p h d", h=SH),
                       bank[i_][0:n, :].rearrange("p (h d) -> p h d", h=SH),
                       tokp[0:n, i_, 8 * j:8 * j + 8].unsqueeze(2).broadcast_to((n, SH, SP_)), ALU.mult
                       ).then_inc(s("xdt_ready"), 1)
            for g in range(2):
                dve.wait_ge(s("cb_done"), g + 1)
                b_ = bank[4 + 3 * g]
                TT(cb[:, g, 0:3 * P], b_[:, 0:3 * P], mask_ssm[:, :], ALU.mult).then_inc(s("cb_ready"), 1)
                TT(cb[0:TS, g, 3 * P:3 * P + TS], b_[0:TS, 3 * P:3 * P + TS], mask_ssms[:, :], ALU.mult
                   ).then_inc(s("cb_ready"), 1)
            dve.wait_ge(s("ecum_spread"), 1)
            dve.tensor_copy(ecum[:, :, :], bank[5][:, 256:512].rearrange("p (c t) -> p c t", c=WC)
                            ).then_inc(s("ecum_copied"), 1)
            for hd in range(SH):
                dve.wait_ge(s("cum_spread"), hd + 1)
                if hd >= 2:
                    dve.wait_ge(s("y_done"), hd - 1)
                b_, sg = bank[hd % 2], seg[:, hd % 2, :]
                for (n, o_, w, i_, t0) in ((P, 0, 2 * P, 0, 0), (P, 2 * P, P, 1, P), (TS, 3 * P, TS, 2, 2 * P)):
                    TSC(sg[0:n, o_:o_ + w], b_[0:n, t0:t0 + w], tokp[0:n, i_, 16 + hd:17 + hd], 0.0,
                        ALU.add, ALU.min).then_inc(s("seg_ready"), 1)
                dve.wait_ge(s("seg_exp"), 2 * (hd + 1))
                g = hd // (SH // 2)
                TT(sg[:, 0:3 * P], sg[:, 0:3 * P], cb[:, g, 0:3 * P], ALU.mult).then_inc(s("w_ready"), 1)
                TT(sg[0:TS, 3 * P:3 * P + TS], sg[0:TS, 3 * P:3 * P + TS], cb[0:TS, g, 3 * P:3 * P + TS],
                   ALU.mult).then_inc(s("w_ready"), 1)
            y = proj[:, TB:TB + WC, :]
            dve.wait_ge(s("y_state_done"), NB)
            dve.wait_ge(s("ecum_copied"), 1)
            dve.wait_ge(s("y_ready"), SH)
            dve.wait_ge(s("h0_ready"), NB)
            ys = h0_t[:, 0, 0:256].rearrange("p (c t) -> p c t", c=WC)
            ch(TT(ys, bank[4][:, 0:256].rearrange("p (c t) -> p c t", c=WC), ecum[:, :, :], ALU.mult))
            ch(TT(y[:, :, SEQ:T], y[:, :, SEQ:T], ys, ALU.add))
            for c in range(WC):
                ch.add(STT(y[:, c, :], proj[:, TX + c, :], d_skip[:, c:c + 1], y[:, c, :], ALU.mult, ALU.add))
            ch.wait()
            dve.wait_ge(s("z_silu"), 1)
            ch(TT(y, y, proj[:, TZ:TZ + WC, :], ALU.mult))
            dve.wait_ge(s("b_tok_ready"), 3)
            for q in range(2):
                if q:
                    dve.wait_ge(s("new_state_done"), WC)
                for b in range(4):
                    TSC(b_own[:, b, :], b_tok[0:TS, 2, :], own_seq[:, 4 * q + b:4 * q + b + 1], None, ALU.mult
                        ).then_inc(s("b_own_ready"), 1)
                for c in range(WC):
                    dve.wait_ge(s("new_state_done"), WC * q + c + 1)
                    for b in range(4):
                        st = states[:, 4 * q + b, c, :]
                        tl = NT * (4 * q + b) + NT - 1
                        ch.add(STT(st, st, ecum[:, c, tl:tl + 1], bank[c][:, P * b:P * (b + 1)], ALU.mult, ALU.add))
                ch.wait()
                dve.sem_inc(s("states_new"), 1)
            dve.wait_ge(s("y_done"), SH)
            dve.wait_ge(s("prompt_state_done"), 1)
            TT(xdt_sq, y, y, ALU.mult).then_inc(s("norm_squared"), 1)
            norm_inverse(2, W)
            for c in range(WC):
                STT(y[:, c, :], y[:, c, :], par_w[:, c, SG:SG + 1], rows[:, 0, :], ALU.mult, ALU.mult
                    ).then_inc(s("ssm_ready"), 1)

            ch(dve.memset(scratch[:, 0:2560], 0.0))
            for e in range(2):
                hf = slice(e * DH, (e + 1) * DH)
                dve.tensor_copy(q_pair[hf, :, :, NT * e:NT * (e + 1)].rearrange("p b c t -> p c b t"),
                                proj[hf, TQ:TQ + WC, SEQ:T].rearrange("p c (b t) -> p c b t", b=NB)
                                ).then_inc(s("q_spread"), 1)
                dve.tensor_copy(q_head[hf, e:H:2, :], proj[hf, TQ:TQ + WC, 0:SEQ]).then_inc(s("q_spread"), 1)
            for u in range(2):
                dve.memset(later[:, u, 448:512], 0.0).then_inc(s("later_zero"), 1)
            dve.wait_ge(s("later_zero"), 2)
            dve.wait_ge(s("zn_log"), 1)
            zn = bank[4][0:TS, :].rearrange("p (b n) -> p b n", b=NB)
            ch(STT(soft_new, zn, 0.0, w_new, ALU.max, ALU.add))
            TT(soft_new, soft_new, mask_new[:, :, :], ALU.mult).then_inc(s("soft_new"), 1)
            dve.wait_ge(s("cn_done"), 1)
            TSC(w_new, zn, 0.0, None, ALU.min).then_inc(s("wn_arg"), 1)
            dve.wait_ge(s("wn_exp"), 1)
            TT(w_new, w_new, mask_new[:, :, :], ALU.mult).then_inc(s("w_new"), 1)
            dve.wait_ge(s("soft_new"), 1)
            dve.sem_inc(s("odd_copied"), 1)
            dve.sem_inc(s("o_copied"), 4)
            with dve.Fori(0, NB // 2) as i:
                ch.begin(i, 2 * (NPAGE - 1))
                for u in range(2):
                    for p in range(1, NPAGE, 2):
                        dve.wait_ge(s("k_page_turned"), i * 16 + (8 * u + p + 1))
                        dve.tensor_copy(k_turn[:, 1, :], bank[1][:, :]).then_inc(s("odd_copied"), 1)
                    dve.wait_ge(s("z_log"), i * 2 + (u + 1))
                    ch.add(STT(soft[:, u, :], bank[2 + u][:, :], 0.0, wgt[:, u, :], ALU.max, ALU.add))
                    dve.tensor_copy(later[0:TS, u, 448:512],
                                    soft_new[:, bass.ds(i * 2 + u, 1), :].rearrange("p b n -> p (b n)")
                                    ).then_inc(s("soft_ready"), 1)
                    dve.wait_ge(s("soft_ready"), i * 4 + (2 * u + 1))
                    ch.wait()
                    for p in range(NPAGE - 2, -1, -1):
                        lt, nx = later[:, u, 64 * p:64 * (p + 1)], slice(64 * (p + 1), 64 * (p + 2))
                        ins = TT(lt, later[:, u, nx], soft[:, u, nx], ALU.add)
                        if p:
                            ch(ins)
                        else:
                            ins.then_inc(s("soft_ready"), 1)
                for u in range(2):
                    dve.wait_ge(s("o_done"), i * 2 + (u + 1))
                    for e in range(2):
                        hf = slice(e * DH, (e + 1) * DH)
                        ins = dve.tensor_copy(att[hf, :, bass.ds(i * (2 * NT) + (SEQ + NT * u), NT)],
                                              bank[5 + u][hf, 0:64].rearrange("p (c k) -> p c k", c=WC)[:, :, NT * e:NT * (e + 1)])
                        ins.then_inc(s("o_copied"), 1)
                ch.end(NB // 2)
            for hd in range(H):
                u, b_h = hd % 2, sb_bias[:, hd:hd + 1]
                sf, wg, z = soft[:, u, 0:3 * P], wgt[:, u, 0:3 * P], bank[u][:, 0:3 * P]
                dve.wait_ge(s("pz_log"), hd + 1)
                ch(TSC(sf, z, b_h, 0.0, ALU.add, ALU.max))
                ch(TT(sf, sf, wg, ALU.add))
                TT(sf, sf, mask_att[:, :], ALU.mult).then_inc(s("p_soft"), 1)
                dve.wait_ge(s("pc_done"), hd + 1)
                TSC(wg, z, b_h, 0.0, ALU.add, ALU.min).then_inc(s("pw_arg"), 1)
                dve.wait_ge(s("pw_exp"), hd + 1)
                TT(wg, wg, mask_att[:, :], ALU.mult).then_inc(s("pw_ready"), 1)

            n_ = 0
            for j, n in enumerate((1, 2, 0)):
                for m in range(DC):
                    dve.wait_ge(s("branch_done"), n_ + 1)
                    b_, g_ = bank[4 + n_ % 4][:, 0:T], gates[:, n * DC + m, :]
                    if j == 0:
                        TT(merged[:, m, :], b_, g_, ALU.mult).then_inc(s("merged"), 1)
                    else:
                        ch(TT(g_, b_, g_, ALU.mult))
                        dve.wait_ge(s("merged"), n_ - 7)
                        TT(merged[:, m, :], merged[:, m, :], g_, ALU.add).then_inc(s("merged"), 1)
                    n_ += 1
            for m in range(DC):
                dve.wait_ge(s("out_done"), m + 1)
                TT(x[:, m, :], x[:, m, :], bank[m % 4][:, 0:T], ALU.add).then_inc(s("out_added"), 1)

            dve.wait_ge(s("out_added"), DC)
            norm_square(3)
            norm_inverse(3, D)
            norm_apply(FFN)
            dve.wait_ge(s("h_ready"), 2 * DC)
            ch(dve.memset(R["logit"], 0.0))
            for i_, (t0, n) in enumerate(BLK):
                dve.wait_ge(s("logits_done"), i_ + 1)
                ch(TT(R["logit"][0:n, i_, :], bank[i_][0:n, 0:NG + NE], router_bias[0:n, :], ALU.add))
            gl, el = R["logit"][:, :, 0:NG], R["logit"][:, :, NG:NG + NE]

            def wide(t, n):
                return t.broadcast_to((P, 3, n))

            def first_max(out, v, top, pri, one):
                ch(dve.tensor_reduce(top, v, AX.X, ALU.max))
                ch(TT(out, v, wide(top, EG), ALU.is_equal))
                ch(TT(pri, out, descend.unsqueeze(1).broadcast_to((P, 3, EG)), ALU.mult))
                ch(dve.tensor_reduce(one, pri, AX.X, ALU.max))
                ch(TT(out, pri, wide(one, EG), ALU.is_equal))

            first_max(R["goh"], gl, R["gmax"], R["gpri"], R["gone"])
            TT(R["gexp"], gl, wide(R["gmax"], NG), ALU.subtract).then_inc(s("g_arg"), 1)
            ch(TT(R["pick"].rearrange("p b (g e) -> p b g e", g=NG), el.rearrange("p b (g e) -> p b g e", g=NG),
                  R["goh"].unsqueeze(3).broadcast_to((P, 3, NG, EG)), ALU.mult))
            ch(dve.tensor_reduce(R["esel"], R["pick"].rearrange("p b (g e) -> p b e g", g=NG), AX.X, ALU.add))
            first_max(R["o1"], R["esel"], R["m1"], R["pri"], R["one"])
            ch(STT(R["esel2"], R["o1"], -1e30, R["esel"], ALU.mult, ALU.add))
            first_max(R["o2"], R["esel2"], R["m2"], R["pri"], R["one"])
            TT(R["w2"], R["m2"], R["m1"], ALU.subtract).then_inc(s("e_arg"), 1)
            dve.wait_ge(s("g_exp"), 1)
            ch(dve.tensor_reduce(R["gsum"], R["gexp"], AX.X, ALU.add))
            dve.wait_ge(s("e_exp"), 1)
            ch(TSC(R["den"], R["w2"], 1.0, None, ALU.add))
            ch(TT(R["den"], R["den"], R["gsum"], ALU.mult))
            ch(dve.reciprocal(R["w1"], R["den"]))
            ch(TT(R["w2"], R["w2"], R["w1"], ALU.mult))
            ch(TT(R["o1"], R["o1"], wide(R["w1"], EG), ALU.mult))
            ch(TT(R["o2"], R["o2"], wide(R["w2"], EG), ALU.mult))
            ch(TT(R["comb4"], R["o1"], R["o2"], ALU.add))
            TT(R["comb"].rearrange("p b (g e) -> p b g e", g=NG), R["goh"].unsqueeze(3).broadcast_to((P, 3, NG, EG)),
               R["comb4"].unsqueeze(2).broadcast_to((P, 3, NG, EG)), ALU.mult).then_inc(s("comb_ready"), 1)

            dve.wait_ge(s("share_ready"), NE)
            dve.sem_inc(s("down_added"), 8)
            with dve.Fori(0, NE // 4) as i:
                ch.begin(i, 16)
                for e in range(4):
                    for m in range(4):
                        t = 4 * e + m
                        dve.wait_ge(s("up_done"), i * 16 + (t + 1))
                        dve.wait_ge(s("silu_ready"), i * 16 + (t + 1))
                        ch(TT(act_t[:, m, :], bank[4 + m][:, 0:T],
                              share[:, bass.ds(i * 4 + e, 1), :].rearrange("p e t -> p (e t)"), ALU.mult))
                        TT(act_t[:, m, :], act_t[:, m, :], silu_t[:, m, :], ALU.mult).then_inc(s("act_ready"), 1)
                    for m in range(DC):
                        dve.wait_ge(s("down_done"), i * 32 + (8 * e + m + 1))
                        TT(x[:, m, :], x[:, m, :], bank[m % 4][:, 0:T], ALU.add).then_inc(s("down_added"), 1)
                ch.end(NE // 4)

            dve.wait_ge(s("down_added"), 8 + DC * NE)
            norm_square(4)
            norm_inverse(4, D)
            norm_apply(PLN)
            for m in range(DC):
                dve.wait_ge(s("pg_ready"), m + 1)
                dve.wait_ge(s("pp_done"), m + 1)
                ch(TT(silu_t[:, m % 4, :], bank[4 + m % 4][:, 0:T], silu_t[:, m % 4, :], ALU.mult))
                TT(x[:, m, :], x[:, m, :], silu_t[:, m % 4, :], ALU.add).then_inc(s("pple_added"), 1)
            dve.wait_ge(s("pple_added"), DC)
            norm_square(5)
            norm_inverse(5, D)
            norm_apply(FIN)
            for i_, (t0, n) in enumerate(BLK):
                dve.wait_ge(s("y_turned"), 2 * i_ + 2)
                dve.tensor_copy(y_tok[0:n, i_, 512:1024], bank[2 * i_ + 1][0:n, :]).then_inc(s("y_high_ready"), 1)

        @block.tensor
        def _(pe):
            MM, TR = pe.matmul, pe.transpose

            pe.wait_ge(s("ident_ready"), 1)
            pe.wait_ge(s("x_loaded"), 32)
            for c in range(DC):
                if c >= 4:
                    pe.wait_ge(s("x_ready"), c - 3)
                for i_, (t0, n) in enumerate(BLK):
                    m = TR(bank[c % 4][:, t0:t0 + n], x_tok[0:n, i_, c * P:(c + 1) * P], ident[0:n, 0:n])
                m.then_inc(s("x_turned"), 1)
            pe.wait_ge(s("par_loaded"), 13 * 16)
            for c in range(DC):
                m = TR(bank[4][:, 33 * c:33 * (c + 1)], raw_d[:, c * P:(c + 1) * P], ident[0:33, 0:33])
            m.then_inc(s("par_turned"), 1)
            n = 4 + KC
            for c in range(WC):
                m = TR(bank[5][:, n * c:n * (c + 1)], raw_w[:, c * P:(c + 1) * P], ident[0:n, 0:n])
            m.then_inc(s("par_turned"), 1)
            pe.wait_ge(s("x_ready"), DC)
            for c in range(WC):
                b_ = bank[6] if c < 2 else bank[3]
                for q in range(2):
                    t0 = 256 * (c % 2) + 120 * q
                    m = TR(b_[:, t0:t0 + 120], raw_cf[:, q, c * P:(c + 1) * P], ident[0:120, 0:120])
            m.then_inc(s("par_turned"), 1)

            def norm_sum(k, src, n):
                for c in range(n):
                    m = MM(bank[7][:, 0:T], ones[:, :], src[:, c, :], start=c == 0, stop=c == n - 1)
                m.then_inc(s("norm_summed"), 1)

            pe.wait_ge(s("const"), 2)
            pe.wait_ge(s("norm_squared"), 2)
            norm_sum(0, h, DC)

            pe.wait_ge(s("par_ready"), 2 + WC)
            pe.wait_ge(s("w_dt_loaded"), 16)
            for k in range(DC):
                pe.wait_ge(s("h_ready"), k + 1)
                m = MM(bank[4][0:SH, 0:T], w_dt[:, k, :], h[:, k, :], start=k == 0, stop=k == DC - 1)
            m.then_inc(s("dt_done"), 1)

            def project(i, first):
                for j in range(2):
                    pe.wait_ge(s(f"w_in_loaded{j}"), i * 16 + (first // 8 * 16 + 16))
                    for t in range(4 * j, 4 * j + 4):
                        pe.wait_ge(s("proj_evac"), i * 8 + (first + t + 1))
                        for k in range(DC):
                            m = MM(bank[t % 4][:, 0:T], slot(j, DC, GROUP)[:, k, (t % 4) * P:(t % 4 + 1) * P],
                                   h[:, k, :], start=k == 0, stop=k == DC - 1)
                        m.then_inc(s("proj_done"), 1)

            with pe.Fori(0, 4) as i:
                project(i, 0)

            def turn(name, b_, src, t0, n, chunks):
                for c in range(chunks):
                    m = TR(b_[0:n, c * P:(c + 1) * P], src(c)[:, t0:t0 + n], ident[:, :])
                m.then_inc(s(name + "_turned"), 1)

            pe.wait_ge(s("proj_evac"), 4 + 32)
            pe.wait_ge(s("x_ready"), DC)
            n_ = 0
            for name, tile in (("k", TK), ("v", TV)):
                for i_, (t0, n) in enumerate(BLK):
                    if n_ >= 2:
                        if n_ - 2 < 3:
                            pe.wait_ge(s("k_tok_ready"), n_ - 1)
                        else:
                            pe.wait_ge(s("v_tok_ready"), n_ - 4)
                    turn(name, bank[5 + n_ % 2], lambda c: proj[:, tile + c, :], t0, n, WC)
                    n_ += 1
            for q in range(2):
                pe.wait_ge(s("v_tok_ready"), 2 + q)
                turn("xbc", bank[5 + q], lambda c: proj[:, TX + 4 * q + c, :], T - P, P, WC)

            with pe.Fori(0, 3) as i:
                project(i, 32)

            pe.wait_ge(s("u_ready"), 1 + WC)
            pe.wait_ge(s("xbc_tok_ready"), 2)
            for c in range(WC):
                TR(bank[5][0:TS, c * P:(c + 1) * P], cpad[:, c, CPAD - TS:CPAD], ident[:, :])
            for c in range(WC):
                m = TR(bank[6][0:TS, c * P:(c + 1) * P], proj[:, TB + c, SEQ:T], ident[:, :])
            m.then_inc(s("u_turned"), 1)
            pe.wait_ge(s("u_tok_ready"), 2)
            pe.wait_ge(s("cconv_done"), 1)
            for c in range(WC):
                m = MM(bank[6][:, 0:T], ones[:, :], proj[:, TA + c, :], start=c == 0, stop=c == WC - 1)
            m.then_inc(s("mean_summed"), 1)
            pe.wait_ge(s("norm_squared"), 3)
            norm_sum(1, h, WC)

            pe.wait_ge(s("rows_ready"), 1)
            pe.wait_ge(s("decay_exp"), 1)
            for i_, (t0, n) in enumerate(BLK):
                for j, r in enumerate((0, 1, 2)):
                    m = TR(bank[5][0:n, 24 * i_ + 8 * j:24 * i_ + 8 * j + 8], rows[0:SH, r, t0:t0 + n],
                           ident[0:SH, 0:SH])
            m.then_inc(s("rows_turned"), 1)
            pe.wait_ge(s("ecum_ready"), 1)
            pe.wait_ge(s("tokp_ready"), 1)
            for c in range(WC):
                m = MM(bank[5][:, 256 + TS * c:256 + TS * (c + 1)], head_of[:, c, :], reset[:, 0:TS], start=True, stop=True)
            m.then_inc(s("ecum_spread"), 1)
            pe.wait_ge(s("xconv_silu"), 1)
            pe.wait_ge(s("proj_evac"), 60)
            for i_, (t0, n) in enumerate(BLK):
                turn("xs", bank[i_], lambda c: proj[:, TX + c, :], t0, n, WC)
            TBB, TCC = TX + WC, TX + WC + 2
            for i_, (t0, n) in enumerate(BLK):
                b0 = 256 * (i_ % 2)
                for g in range(2):
                    m = TR(bank[3 + 3 * (i_ // 2)][0:n, b0 + P * g:b0 + P * (g + 1)], proj[:, TBB + g, t0:t0 + n], ident[:, :])
                m.then_inc(s("b_turned"), 1)
            pe.wait_ge(s("ln_scaled"), 1)
            for g in range(2):
                b_, B_, C_ = bank[4 + 3 * g], proj[:, TBB + g, :], proj[:, TCC + g, :]
                MM(b_[:, 0:2 * P], B_[:, 0:P], C_[:, 0:SEQ], start=True, stop=True)
                MM(b_[:, 2 * P:3 * P], B_[:, P:SEQ], C_[:, P:SEQ], start=True, stop=True)
                MM(b_[0:TS, 3 * P:3 * P + TS], B_[:, SEQ:T], C_[:, SEQ:T], start=True, stop=True
                   ).then_inc(s("cb_done"), 1)

            def spread_cum(hd):
                MM(bank[hd % 2][:, 0:T], head_row[:, hd, :], rows[0:SH, 2, :], start=True, stop=True
                   ).then_inc(s("cum_spread"), 1)

            pe.wait_ge(s("xdt_ready"), 6)
            pe.wait_ge(s("b_tok_ready"), 3)
            spread_cum(0)
            spread_cum(1)
            for hd in range(SH):
                c = hd // 2
                pe.wait_ge(s("w_ready"), 2 * (hd + 1))
                if hd >= 2:
                    pe.wait_ge(s("y_ready"), hd - 1)
                b_, sg = bank[2 + hd % 2], seg[:, hd % 2, :]
                MM(b_[:, 0:SEQ], xdt[:, 0, c * P:(c + 1) * P], sg[:, 0:SEQ], start=True, stop=False)
                MM(b_[:, P:SEQ], xdt[:, 1, c * P:(c + 1) * P], sg[:, SEQ:SEQ + P], start=False, stop=True)
                MM(b_[:, SEQ:T], xdt[0:TS, 2, c * P:(c + 1) * P], sg[0:TS, 3 * P:3 * P + TS], start=True, stop=True
                   ).then_inc(s("y_done"), 1)
                if hd + 2 < SH:
                    spread_cum(hd + 2)
            pe.wait_ge(s("states_loaded"), 16)
            pe.wait_ge(s("cb_ready"), 4)

            def turn_state(b):
                if b >= 2:
                    pe.wait_ge(s("h0_ready"), b - 1)
                for c in range(WC):
                    m = TR(bank[6 + b % 2][:, c * P:(c + 1) * P], states[:, b, c, :], ident[:, :])
                m.then_inc(s("h0_turned"), 1)

            turn_state(0)
            for b in range(NB):
                if b + 1 < NB:
                    turn_state(b + 1)
                pe.wait_ge(s("h0_ready"), b + 1)
                for c in range(WC):
                    m = MM(bank[4][:, TS * c + NT * b:TS * c + NT * (b + 1)], h0_t[:, b % 2, c * P:(c + 1) * P],
                           proj[:, TCC + c // 2, SEQ + NT * b:SEQ + NT * (b + 1)], start=True, stop=True)
                m.then_inc(s("y_state_done"), 1)
            pe.wait_ge(s("ecum_copied"), 1)
            for c in range(WC):
                for i_ in range(2):
                    m = MM(bank[5][:, c * P:(c + 1) * P], xdec[:, i_, c * P:(c + 1) * P],
                           b_tok[:, i_, (c // 2) * P:(c // 2 + 1) * P], start=i_ == 0, stop=i_ == 1)
            m.then_inc(s("prompt_state_done"), 1)
            pe.wait_ge(s("y_ready"), SH)
            for q in range(2):
                pe.wait_ge(s("b_own_ready"), 4 * (q + 1))
                for c in range(WC):
                    MM(bank[c][:, :], xdec[0:TS, 2, c * P:(c + 1) * P], b_own[:, :, (c // 2) * P:(c // 2 + 1) * P],
                       start=True, stop=True).then_inc(s("new_state_done"), 1)
            pe.wait_ge(s("norm_squared"), 4)
            norm_sum(2, xdt_sq, WC)

            pe.wait_ge(s("states_new"), 2)
            pe.wait_ge(s("prompt_state_ready"), 1)
            pe.wait_ge(s("ssm_ready"), WC)
            pe.wait_ge(s("q_spread"), 4)
            pe.wait_ge(s("bias_row_ready"), 1)
            pe.wait_ge(s("masks"), 1)
            bias2 = bias_row[:, :, :].rearrange("p a n -> p (a n)")
            MM(bank[4][0:TS, :], row0[:, 0:TS], bias2, start=True, stop=False)
            for c in range(WC):
                m = MM(bank[4][0:TS, :].rearrange("p (b n) -> p b n", b=NB)[:, :, 16 * c:16 * (c + 1)],
                       proj[:, TK + c, SEQ:T], q_pair[:, :, c, :], start=False, stop=c == WC - 1)
            m.then_inc(s("zn_done"), 1)
            pe.wait_ge(s("soft_new"), 1)
            MM(bank[4][0:TS, :], neg_tri[0:TS, 0:TS], soft_new.rearrange("p b n -> p (b n)"), start=False, stop=True,
               skip_group_check=True).then_inc(s("cn_done"), 1)
            pe.wait_ge(s("w_new"), 1)

            with pe.Fori(0, NB // 2) as i:
                for u in range(2):
                    kp = slot((2, 0)[u], NPAGE, W)
                    copied = (s("even_copied"), s("odd_copied"))

                    def turn_page(p):
                        pe.wait_ge(copied[p % 2], i * 8 + (4 * u + p // 2 + 1))
                        for c in range(WC):
                            m = TR(bank[p % 2][:, c * P:(c + 1) * P], kp[:, p, c * P:(c + 1) * P], ident[:, :])
                        m.then_inc(s("k_page_turned"), 1)

                    MM(bank[2 + u][:, :], row0[:, :], bias2, start=True, stop=False)
                    pe.wait_ge(s(f"k_loaded{u}"), i * 128 + 128)
                    turn_page(0)
                    for p in range(NPAGE):
                        if p + 1 < NPAGE:
                            turn_page(p + 1)
                        pe.wait_ge(copied[p % 2], i * 8 + (4 * u + p // 2 + 2))
                        for c in range(WC):
                            m = MM(bank[2 + u][:, 64 * p + 16 * c:64 * p + 16 * (c + 1)], k_turn[:, p % 2, c * P:(c + 1) * P],
                                   q_pair[:, bass.ds(i * 2 + u, 1), c, :].rearrange("p b k -> p (b k)"),
                                   start=False, stop=p == NPAGE - 1 and c == WC - 1)
                    m.then_inc(s("z_done"), 1)
                for u in range(2):
                    pe.wait_ge(s("soft_ready"), i * 4 + (2 * u + 2))
                    MM(bank[2 + u][:, :], neg_tri[:, :], soft[:, u, :], start=False, stop=False, skip_group_check=True)
                    MM(bank[2 + u][:, :], neg_ones[:, :], later[:, u, :], start=False, stop=True,
                       skip_group_check=True).then_inc(s("c_done"), 1)
                for u in range(2):
                    vp = slot((3, 1)[u], NPAGE, W)
                    pe.wait_ge(s("wgt_ready"), i * 2 + (u + 1))
                    pe.wait_ge(s(f"v_loaded{u}"), i * 128 + 128)
                    pe.wait_ge(s("o_copied"), i * 4 + (2 * u + 2))
                    for c in range(WC):
                        for p in range(NPAGE):
                            MM(bank[5 + u][:, 16 * c:16 * (c + 1)], vp[:, p, c * P:(c + 1) * P],
                               wgt[:, u, 64 * p + 16 * c:64 * p + 16 * (c + 1)], start=p == 0, stop=False)
                        m = MM(bank[5 + u][:, 16 * c:16 * (c + 1)], v_tok[0:TS, 2, c * P:(c + 1) * P],
                               w_new[:, bass.ds(i * 2 + u, 1), 16 * c:16 * (c + 1)].rearrange("p b k -> p (b k)"),
                               start=False, stop=True)
                    m.then_inc(s("o_done"), 1)

            def p_scores(hd):
                z, c = bank[hd % 2], hd // 2
                MM(z[:, 0:SEQ], proj[:, TK + c, 0:P], q_head[:, hd, :], start=True, stop=True)
                MM(z[:, SEQ:3 * P], proj[:, TK + c, P:SEQ], q_head[:, hd, P:SEQ], start=False, stop=True,
                   skip_group_check=True).then_inc(s("pz_done"), 1)

            def p_out(hd):
                o_, c, wg = bank[2 + hd % 2], hd // 2, wgt[:, hd % 2, :]
                pe.wait_ge(s("pw_ready"), hd + 1)
                if hd >= 2:
                    pe.wait_ge(s("att_ready"), hd - 1)
                MM(o_[:, 0:SEQ], v_tok[:, 0, c * P:(c + 1) * P], wg[:, 0:SEQ], start=True, stop=False)
                MM(o_[:, P:SEQ], v_tok[:, 1, c * P:(c + 1) * P], wg[:, SEQ:3 * P], start=False, stop=True
                   ).then_inc(s("po_done"), 1)

            pe.wait_ge(s("even_copied"), 33)
            pe.wait_ge(s("odd_copied"), 33)
            p_scores(0)
            for hd in range(H):
                z, sf = bank[hd % 2], soft[:, hd % 2, :]
                if hd >= 1:
                    p_out(hd - 1)
                if hd + 1 < H:
                    p_scores(hd + 1)
                pe.wait_ge(s("p_soft"), hd + 1)
                MM(z[:, 0:3 * P], neg_tri[:, :], sf[:, 0:3 * P], start=False, stop=False, skip_group_check=True)
                MM(z[:, P:SEQ], neg_ones[:, :], sf[:, SEQ:3 * P], start=False, stop=True,
                   skip_group_check=True).then_inc(s("pc_done"), 1)
            p_out(H - 1)

            pe.wait_ge(s("o_copied"), 4 + 2 * NB)
            n_, L = 0, 0
            for n in (1, 2, 0):
                src = {0: att, 1: proj[:, TB:TB + WC, :], 2: proj[:, TA:TA + WC, :]}[n]
                if n == 0:
                    pe.wait_ge(s("att_ready"), H)
                loaded(pe, L)
                for m_ in range(DC):
                    if n_ >= 4:
                        pe.wait_ge(s("merged"), n_ - 3)
                    for k in range(WC):
                        m = MM(bank[4 + n_ % 4][:, 0:T], slot(L % 4, WC, D)[:, k, m_ * P:(m_ + 1) * P], src[:, k, :],
                               start=k == 0, stop=k == WC - 1)
                    m.then_inc(s("branch_done"), 1)
                    n_ += 1
                L += 1
            pe.wait_ge(s("merged"), 3 * DC)
            for j in range(2):
                loaded(pe, L)
                for m_ in range(4):
                    if j:
                        pe.wait_ge(s("out_added"), m_ + 1)
                    for k in range(DC):
                        m = MM(bank[m_][:, 0:T], slot(L % 4, DC, GROUP)[:, k, m_ * P:(m_ + 1) * P], merged[:, k, :],
                               start=k == 0, stop=k == DC - 1)
                    m.then_inc(s("out_done"), 1)
                L += 1

            pe.wait_ge(s("norm_squared"), 6)
            norm_sum(3, h, DC)
            pe.wait_ge(s("h_ready"), 2 * DC)
            pe.wait_ge(s("small_loaded"), 9 * 16)
            for i_, (t0, n) in enumerate(BLK):
                for k in range(DC):
                    m = MM(bank[i_][0:n, 0:NG + NE], h[:, k, t0:t0 + n], w_router[:, k, :], start=k == 0, stop=k == DC - 1)
                m.then_inc(s("logits_done"), 1)
            pe.wait_ge(s("comb_ready"), 1)
            for i_, (t0, n) in enumerate(BLK):
                m = TR(bank[3][0:NE, t0:t0 + n], R["comb"][0:n, i_, :], ident[0:n, 0:n])
            m.then_inc(s("comb_turned"), 1)
            pe.wait_ge(s("share_row_ready"), 1)
            pe.wait_ge(s("expert_row_ready"), 1)
            for e in range(NE):
                if e >= 4:
                    pe.wait_ge(s("share_ready"), e - 3)
                MM(bank[4 + e % 4][:, 0:T], expert_row[:, e, :], share_row, start=True, stop=True
                   ).then_inc(s("share_spread"), 1)
            pe.wait_ge(s("share_ready"), NE)

            with pe.Fori(0, NE // 4) as i:
                for e in range(4):
                    for r, name in enumerate(("gate", "up")):
                        loaded(pe, L + 3 * e + r, i, 12)
                        for m_ in range(4):
                            if r == 0:
                                pe.wait_ge(s("down_added"), i * 32 + (8 * e + m_ + 5))
                            for k in range(DC):
                                m = MM(bank[4 * r + m_][:, 0:T], slot((L + 3 * e + r) % 4, DC, DE)[:, k, m_ * P:(m_ + 1) * P],
                                       h[:, k, :], start=k == 0, stop=k == DC - 1)
                            m.then_inc(s(name + "_done"), 1)
                            loaded(pe, L + 3 * e + 2, i, 12)
                    for m_ in range(DC):
                        if m_ >= 4:
                            pe.wait_ge(s("down_added"), i * 32 + (8 * e + m_ + 5))
                        for k in range(DE // P):
                            if m_ == 0:
                                pe.wait_ge(s("act_ready"), i * 16 + (4 * e + k + 1))
                            m = MM(bank[m_ % 4][:, 0:T], slot((L + 3 * e + 2) % 4, DE // P, D)[:, k, m_ * P:(m_ + 1) * P],
                                   act_t[:, k, :], start=k == 0, stop=k == DE // P - 1)
                        m.then_inc(s("down_done"), 1)
                L += 3 * NE

            pe.wait_ge(s("p_loaded"), 32)
            for i_, (t0, n) in enumerate(BLK):
                for c in range(PLE // P):
                    m = TR(bank[4 + c][:, t0:t0 + n], p_tok[0:n, i_, c * P:(c + 1) * P], ident[0:n, 0:n])
            m.then_inc(s("p_turned"), 1)
            pe.wait_ge(s("norm_squared"), 8)
            norm_sum(4, h, DC)
            pe.wait_ge(s("h_ready"), 3 * DC)
            pe.wait_ge(s("p_ready"), 2)
            loaded(pe, L + 2)
            for m_ in range(DC):
                if m_ % 4 == 0:
                    loaded(pe, L + m_ // 4)
                if m_ >= 4:
                    pe.wait_ge(s("pple_added"), m_ - 3)
                for k in range(DC):
                    m = MM(bank[m_ % 4][:, 0:T], slot((L + m_ // 4) % 4, DC, GROUP)[:, k, (m_ % 4) * P:(m_ % 4 + 1) * P],
                           h[:, k, :], start=k == 0, stop=k == DC - 1)
                m.then_inc(s("pg_done"), 1)
                for k in range(PLE // P):
                    m = MM(bank[4 + m_ % 4][:, 0:T], slot((L + 2) % 4, PLE // P, D)[:, k, m_ * P:(m_ + 1) * P],
                           p_feat[:, k, :], start=k == 0, stop=k == PLE // P - 1)
                m.then_inc(s("pp_done"), 1)

            pe.wait_ge(s("norm_squared"), 10)
            norm_sum(5, h, DC)
            pe.wait_ge(s("h_ready"), 4 * DC)
            for i_, (t0, n) in enumerate(BLK):
                for q in range(2):
                    for c in range(4):
                        m = TR(bank[2 * i_ + q][0:n, c * P:(c + 1) * P], h[:, 4 * q + c, t0:t0 + n], ident[:, :])
                    m.then_inc(s("y_turned"), 1)


_INS = ["x_prompt", "x_sample", "p_prompt", "p_sample", "cache_k", "cache_v", "page_table",
        "state_ssm", "state_ssm_conv", "state_cf_conv", "norm_mix", "w_in", "sb_bias",
        "ssm_conv_w", "ssm_conv_b", "dt_bias", "a_log", "d_skip", "ssm_norm",
        "cf_conv_w", "cf_conv_b", "cf_ln_g", "cf_ln_b", "w_branch", "w_out",
        "norm_ffn", "w_router_group", "b_router_group", "w_router_expert", "b_router_expert",
        "w_expert_gate", "w_expert_up", "w_expert_down", "norm_ple", "w_ple_gate", "w_ple_proj",
        "norm_final"]
_OUTS = [("y_prompt", (1, 256, 1024)), ("y_sample", (8, 8, 1024)),
         ("k_prompt", (1, 1, 256, 8, 64)), ("v_prompt", (1, 1, 256, 8, 64)),
         ("ssm_prompt", (1, 1, 8, 64, 128)), ("ssm_conv_prompt", (1, 1, 3, 1024)),
         ("cf_conv_prompt", (1, 1, 30, 512)),
         ("k_sample", (1, 8, 8, 8, 64)), ("v_sample", (1, 8, 8, 8, 64)),
         ("ssm_sample", (1, 8, 8, 64, 128)), ("ssm_conv_sample", (1, 8, 3, 1024)),
         ("cf_conv_sample", (1, 8, 30, 512))]


def kernel(**inputs):
    import numpy as _np
    import concourse.bacc as _bacc
    from concourse import mybir as _mybir
    from concourse.bass_utils import run_bass_kernel_spmd as _run

    nc = _bacc.Bacc("TRN2", target_bir_lowering=False, num_devices=1)
    arrays, ins, outs = {}, {}, {}
    for name in _INS:
        arr = _np.ascontiguousarray(inputs[name])
        arrays[f"in_{name}"] = arr
        ins[name] = nc.dram_tensor(f"in_{name}", arr.shape, _mybir.dt.from_np(arr.dtype), kind="ExternalInput").ap()
    for name, shape in _OUTS:
        outs[name] = nc.dram_tensor(f"out_{name}", shape, _mybir.dt.float32, kind="ExternalOutput").ap()
    build(nc, ins, outs)
    r = _run(nc, [arrays], core_ids=[0])
    return tuple(r.results[0][f"out_{name}"] for name, _ in _OUTS)
```

```python
from contextlib import ExitStack

import concourse.bass as bass
from concourse import mybir

F32 = mybir.dt.float32
I32 = mybir.dt.int32
ALU = mybir.AluOpType
ACT = mybir.ActivationFunctionType
AX = mybir.AxisListType

P = 128


class Chain:

    def __init__(self, eng, sem):
        self.eng, self.sem, self.n, self.i, self.per = eng, sem, 0, None, 0

    def begin(self, i, per):
        self.i, self.per, self.first = i, per, self.n

    def end(self, turns):
        assert self.n - self.first == self.per, (self.n - self.first, self.per)
        self.n += self.per * (turns - 1)
        self.i = None

    def add(self, ins):
        ins.then_inc(self.sem, 1)
        self.n += 1

    def wait(self):
        self.eng.wait_ge(self.sem, self.n if self.i is None else self.i * self.per + self.n)

    def __call__(self, ins):
        self.add(ins)
        self.wait()


def build(nc, a, o):
    _, SEQ, D = a["x_prompt"].shape
    NB, NT, _ = a["x_sample"].shape
    PLE = a["p_prompt"].shape[-1]
    _, POOL, PAGE, H, DH = a["cache_k"].shape
    NPAGE = a["page_table"].shape[1]
    W = H * DH
    _, _, SH, SP_, SN = a["state_ssm"].shape
    KS = a["ssm_conv_w"].shape[1]
    XC = a["ssm_conv_w"].shape[2]
    KC = a["cf_conv_w"].shape[1]
    NE, _, DE = a["w_expert_gate"].shape[1:]
    NG = a["w_router_group"].shape[2]
    EG = NE // NG
    TS = NB * NT
    T = SEQ + TS
    DC, WC, XCC = D // P, W // P, XC // P
    EPS = 1e-6
    BLK = [(0, P), (P, P), (2 * P, TS)]
    assert SEQ == 2 * P and TS == 64 and NB == 8 and NT == 8 and PAGE == P and DH == 64
    assert D == 1024 and W == 512 and XC == 1024 and SN == P and SP_ == 64 and NPAGE == 8
    COL_DT = 4 * W + XC
    COL_GLU = COL_DT + SH
    GROUP = 512
    TQ, TK, TV, TZ, TX, TA, TB = 0, 4, 8, 12, 16, 24, 28

    w_in_v = a["w_in"][0].rearrange("(k p) n -> p k n", p=P)

    with ExitStack() as ctx:
        def sb(name, shape, dt=F32):
            return ctx.enter_context(nc.sbuf_tensor(name, shape, dt))

        def sem(name):
            return ctx.enter_context(nc.semaphore(name))

        ring = sb("ring", [P, 4, 4096])
        proj = sb("proj", [P, 32, T])
        gates = sb("gates", [P, 3 * DC, T])
        x = sb("x", [P, DC, T])
        scratch = sb("scratch", [P, 7696])
        v_tok = sb("v_tok", [P, 3, W])
        att = sb("att", [P, WC, T])
        rows = sb("rows", [P, 3, T])
        reset = sb("reset", [SH, T])
        ident = sb("ident", [P, P])
        ones = sb("ones", [P, P])
        neg_tri = sb("neg_tri", [P, P])
        neg_ones = sb("neg_ones", [P, P])
        row0 = sb("row0", [P, P])
        mask_att = sb("mask_att", [P, 3 * P])
        mask_ssm = sb("mask_ssm", [P, 3 * P])
        mask_ssms = sb("mask_ssms", [TS, TS])
        mask_new = sb("mask_new", [TS, NB, H * NT])
        bias_row = sb("bias_row", [P, NPAGE, H * NT])
        head_of = sb("head_of", [SH, WC, P])
        own_seq = sb("own_seq", [TS, NB])
        count_to = sb("count_to", [P, P])
        crowded = sb("crowded", [1, 1], I32)
        eps = sb("eps", [P, 1])
        par_d = sb("par_d", [P, DC, 33])
        par_w = sb("par_w", [P, WC, 4 + KC])
        small = sb("small", [P, 40])
        pages = sb("pages", [1, NB * NPAGE], I32)
        w_router = sb("w_router", [P, DC, NG + NE])

        MIX, FFN, PLN, FIN, CW, CB, CS = 0, 1, 2, 3, 4, 8, 9
        SG, CFB, LNG, LNB, CFW = 0, 1, 2, 3, 4
        sb_bias = small[:, 0:8]
        d_skip = small[:, 8:12]
        router_bias = small[:, 16:16 + NG + NE]
        descend = small[:, 36:36 + EG]
        dt_bias, a_log, e_a = small[0:SH, 12:13], small[0:SH, 13:14], small[0:SH, 14:15]

        h = scratch[:, 0:DC * T].rearrange("p (c t) -> p c t", t=T)
        XPAD, CPAD = SEQ + KS - 1, SEQ + KC - 1
        xw_ = XPAD + NB * (NT + KS - 1)
        cw_ = CPAD + NB * (NT + KC - 1)
        o1 = DC * T
        o2 = o1 + XCC * xw_
        assert o2 + WC * cw_ == 7696
        xpad = scratch[:, o1:o2].rearrange("p (c t) -> p c t", t=xw_)
        cpad = scratch[:, o2:o2 + WC * cw_].rearrange("p (c t) -> p c t", t=cw_)
        xpad_s = [xpad[:, c, XPAD:xw_].rearrange("p (b t) -> p b t", b=NB) for c in range(XCC)]
        cpad_s = [cpad[:, c, CPAD:cw_].rearrange("p (b t) -> p b t", b=NB) for c in range(WC)]

        def slot(s, *shape):
            n = 1
            for d_ in shape:
                n *= d_
            v = ring[:, s, 0:n]
            if len(shape) == 2:
                v = v.rearrange("p (k n) -> p k n", k=shape[0])
            return v

        def loaded(eng, L, i=0, per=0):
            v = 16 * (L // 4 + 1)
            eng.wait_ge(s(f"ring_loaded{L % 4}"), i * (16 * per // 4) + v if per else v)

        x_tok = slot(2, 3, D)
        raw_d = ring[0:33, 3, 0:1024]
        raw_w = ring[0:4 + KC, 3, 1024:1536]
        raw_cf = ring[0:120, 3, 1536:2560].rearrange("p (a c) -> p a c", a=2)
        k_tok = ring[:, 2, 0:3 * W].rearrange("p (b n) -> p b n", b=3)
        xbc_tok = ring[:, 2, 1536:2560]
        u_tok = ring[0:TS, 2, 2560:3584].rearrange("p (g n) -> p g n", g=2)
        states = ring[:, 3, :].rearrange("p (b c n) -> p b c n", b=NB, c=WC)

        def part(off, *shape):
            n = 1
            for d_ in shape:
                n *= d_
            v = scratch[:, off:off + n]
            return v if len(shape) == 1 else v.rearrange("p (k n) -> p k n", k=shape[0])
        xdt, xdec = part(0, 3, W), part(1536, 3, W)
        b_tok = part(3072, 3, 2 * SN)
        cb = part(3840, 2, 3 * P + TS)
        seg = part(4736, 2, 3 * P + TS)
        b_own = part(3840, 4, 2 * SN)[0:TS]
        h0_t = part(5632, 2, 4 * P)
        ecum = part(6656, WC, TS)
        tokp = part(6912, 3, 24)
        prompt_state = part(6984, WC, SN)
        xdt_sq = part(0, WC, T)

        q_head = part(0, H, SEQ)
        q_pair = scratch[:, 2048:2560].rearrange("p (b c k) -> p b c k", b=NB, c=WC)
        k_turn = part(2560, 2, 512)
        soft = part(3584, 2, 512)
        later = part(4608, 2, 512)
        wgt = part(5632, 2, 512)
        w_new = scratch[0:TS, 7168:7680].rearrange("p (b n) -> p b n", b=NB)
        soft_new = rows[:, :, :].rearrange("p a t -> p (a t)")[0:TS, 0:512].rearrange("p (b n) -> p b n", b=NB)
        expert_row = scratch[0:NE, 3072:5120].rearrange("p (e n) -> p e n", e=NE)
        share = gates[:, 0:NE, :]
        share_row = proj[0:NE, 24, :]
        silu_t, act_t = proj[:, 16:20, :], proj[:, 20:24, :]
        merged = proj[:, 0:DC, :]
        p_tok = v_tok[:, :, 0:PLE]
        p_feat = proj[:, 28:28 + PLE // P, :]
        y_tok = slot(0, 3, D)
        CAP = P
        grid = gates[:, :, :].rearrange("p c t -> p (c t)")
        h_tok = grid[:, 0:3 * D].rearrange("p (b n) -> p b n", b=3)
        h_exp = grid[:, 3072:5120].rearrange("p (u n) -> p u n", u=2)
        pick_t = grid[:, 5120:5888].rearrange("p (u b n) -> p u b n", u=2, b=3)
        weigh_t = grid[:, 5888:6656].rearrange("p (u b n) -> p u b n", u=2, b=3)
        y_exp = grid[:, 6656:7680]
        half = proj[:, 0:8, :].rearrange("p c t -> p (c t)")
        silu_s, act_s, act_ft = half[:, 0:DE], half[:, DE:2 * DE], half[:, 2 * DE:3 * DE]
        weigh_s = half[:, 3 * DE:3 * DE + 2 * T].rearrange("p (u t) -> p u t", u=2)
        flat = att[:, :, :].rearrange("p c t -> p (c t)")
        slot_no = flat[:, 0:3 * NE].rearrange("p (b e) -> p b e", b=3)
        most = flat[0:1, 64:65]
        taken, rank, one_row = rows[0:NE, 0, :], rows[0:NE, 1, :], rows[0:NE, 2, :]
        R = {}
        off = 2560
        for name, n in (("logit", NG + NE), ("gmax", 1), ("gexp", NG), ("gsum", 1), ("goh", NG), ("gpri", NG),
                        ("gone", 1), ("pick", NE), ("esel", EG), ("m1", 1), ("o1", EG), ("pri", EG), ("one", 1),
                        ("m2", 1), ("o2", EG), ("w1", 1), ("w2", 1), ("den", 1), ("esel2", EG), ("comb4", EG), ("comb", NE)):
            R[name] = scratch[:, off:off + 3 * n].rearrange("p (b n) -> p b n", b=3)
            off += 3 * n
        assert off <= 3072
        w_dt = gates[:, 0, 0:DC * SH].rearrange("p (k n) -> p k n", k=DC)
        head_row = att[0:SH, :, :].rearrange("p c t -> p (c t)")[:, 0:SH * P].rearrange(
            "p (h n) -> p h n", n=P)

        bank = [ctx.enter_context(nc.psum_tensor(f"bank{i}", [P, 512], F32)) for i in range(8)]

        S = {}

        def s(name):
            if name not in S:
                S[name] = sem(name)
            return S[name]

        block = ctx.enter_context(nc.Block())

        @block.sync
        def _(sp):
            sp.dma_start(x_tok[:, 0:2, :], a["x_prompt"][0].rearrange("(b p) d -> p b d", p=P)
                         ).then_inc(s("x_loaded"), 16)
            sp.dma_start(x_tok[0:TS, 2, :], a["x_sample"].rearrange("b t d -> (b t) d")
                         ).then_inc(s("x_loaded"), 16)
            sp.dma_start(w_dt, w_in_v[:, :, COL_DT:COL_GLU]).then_inc(s("w_dt_loaded"), 16)

            def w_group(j, col):
                sp.dma_start(slot(j, DC, GROUP), w_in_v[:, :, col]).then_inc(s(f"w_in_loaded{j}"), 16)

            for j in range(2):
                w_group(j, slice(j * GROUP, (j + 1) * GROUP))
            with sp.Fori(1, COL_DT // GROUP // 2) as i:
                for j in range(2):
                    sp.wait_ge(s("proj_done"), i * 8 + (4 * j - 4))
                    w_group(j, bass.ds((i * 2 + j) * GROUP, GROUP))
            sp.wait_ge(s("par_turned"), 3)
            sp.dma_start(states, a["state_ssm"][0].rearrange("b (c e) p n -> (e p) b c n", e=2)
                         ).then_inc(s("states_loaded"), 16)
            with sp.Fori(0, (2 * W + 3 * D) // GROUP // 2) as i:
                for j in range(2):
                    sp.wait_ge(s("proj_done"), i * 8 + (20 + 4 * j))
                    w_group(j, bass.ds((i * 2 + j) * GROUP + COL_GLU, GROUP))

            sp.wait_ge(s("pages_loaded"), 16)

            def sequence(u, b):
                for which, cache in (("k", a["cache_k"]), ("v", a["cache_v"])):
                    dst = slot((2, 0)[u] + (which == "v"), NPAGE, W)
                    if which == "k":
                        regs = [sp.value_load(pages[0:1, bass.ds(b * NPAGE + p, 1)], min_val=0, max_val=POOL - 1)
                                for p in range(NPAGE)]
                    for p in range(NPAGE):
                        sp.dma_start(dst[:, p, :],
                                     cache[0][bass.ds(regs[p], 1)].rearrange("n s h d -> (n s) (h d)")
                                     ).then_inc(s(f"{which}_loaded{u}"), 16)

            sp.wait_ge(s("slot2_stored"), 1)
            sp.wait_ge(s("slot3_stored"), 1)
            sequence(0, 0)
            sp.wait_ge(s("proj_done"), 56)
            sequence(1, 1)
            with sp.Fori(1, NB // 2) as i:
                for u in range(2):
                    sp.wait_ge(s("k_page_turned"), i * 16 + (8 * u - 8))
                    sp.wait_ge(s("o_done"), i * 2 + (u - 1))
                    sequence(u, i * 2 + u)

            def ring_load(L, dst, src):
                sp.dma_start(dst, src).then_inc(s(f"ring_loaded{L % 4}"), 16)

            def halves(w, j):
                return w[0].rearrange("(k p) n -> p k n", p=P)[:, :, j * GROUP:(j + 1) * GROUP]

            def expert(L, e, r, turns_free):
                w, k, n = (("w_expert_gate", DC, DE), ("w_expert_up", DC, DE), ("w_expert_down", DE // P, D))[r]
                sem_, v = turns_free
                sp.wait_ge(s(sem_), v)
                ring_load(L, slot(L % 4, k, n), a[w][0][bass.ds(e, 1)].rearrange("e (k p) n -> p (e k) n", p=P))

            sp.wait_ge(s("k_page_turned"), 8 * NB)
            sp.wait_ge(s("o_done"), NB)
            for L, n in enumerate((1, 2, 0)):
                ring_load(L, slot(L % 4, WC, D), a["w_branch"][0, n].rearrange("(k p) n -> p k n", p=P))
            ring_load(3, slot(3, DC, GROUP), halves(a["w_out"], 0))
            sp.wait_ge(s("branch_done"), DC)
            ring_load(4, slot(0, DC, GROUP), halves(a["w_out"], 1))
            sp.wait_ge(s("po_done"), H)
            sp.dma_start(p_tok[:, 0:2, :], a["p_prompt"][0, 0].rearrange("(b p) n -> p b n", p=P)).then_inc(s("p_loaded"), 16)
            sp.dma_start(p_tok[0:TS, 2, :], a["p_sample"][0].rearrange("b t n -> (b t) n")).then_inc(s("p_loaded"), 16)
            first = [("branch_done", 2 * DC), ("branch_done", 3 * DC), ("out_done", 4), ("out_done", DC)]
            for n in range(4):
                expert(5 + n, n // 3, n % 3, first[n])

            def experts(gate, up, down, per):
                sems = (down, gate, up)

                def turn(i, n0):
                    for n in range(n0, 12):
                        e, r = n // 3, n % 3
                        back = e - 1 if r == 0 else e
                        expert(5 + n, i * 4 + e, r, (sems[r], i * (4 * per[r]) + back * per[r]))
                turn(0, 4)
                with sp.Fori(1, NE // 4) as i:
                    turn(i, 0)
                L = 5 + 3 * NE
                for j, back in enumerate((NE - 1, NE, NE)):
                    sp.wait_ge(s(sems[j]), per[j] * back)
                    if j < 2:
                        ring_load(L + j, slot((L + j) % 4, DC, GROUP), halves(a["w_ple_gate"], j))
                ring_load(L + 2, slot((L + 2) % 4, PLE // P, D), a["w_ple_proj"][0].rearrange("(k p) n -> p k n", p=P))

            sp.wait_ge(s("crowded_ready"), 1)
            with sp.If(sp.value_load(crowded[:, :], min_val=0, max_val=1) == 0):
                experts("gate_done", "up_done", "down_done", (1, 1, 1))
            with sp.Else():
                experts("gate_done", "up_done", "down_done", (DC, 4, 4))

        @block.gpsimd
        def _(pool):
            ch = Chain(pool, s("pool_chain"))

            def where(t, pattern, base, cm, op, fill):
                return pool.affine_select(out=t, in_=t, compare_op=op, fill=fill, base=base,
                                          pattern=pattern, channel_multiplier=cm)

            pool.memset(eps[:, :], EPS).then_inc(s("const"), 1)
            ch(pool.memset(ident[:, :], 0.0))
            where(ident[:, :], [[-1, P]], 0, 1, ALU.not_equal, 1.0).then_inc(s("ident_ready"), 1)
            pool.memset(ones[:, :], 1.0).then_inc(s("const"), 1)
            pool.memset(xpad[:, :, 0:KS - 1], 0.0).then_inc(s("const"), 1)
            pool.memset(cpad[:, :, 0:KC - 1], 0.0).then_inc(s("const"), 1)
            ch.add(pool.memset(neg_ones[:, :], -1.0))
            ch.add(pool.memset(neg_tri[:, :], -1.0))
            ch.add(pool.memset(row0[:, :], 1.0))
            ch.add(pool.memset(mask_att[:, :], 1.0))
            ch.add(pool.memset(mask_ssm[:, :], 1.0))
            ch.add(pool.memset(mask_ssms[:, :], 1.0))
            ch.add(pool.memset(mask_new[:, :, :], 1.0))
            ch.add(pool.memset(reset[:, :], 1.0))
            for j in range(EG):
                ch.add(pool.memset(descend[:, j:j + 1], float(EG - j)))
            ch.add(pool.memset(bias_row[:, :, :], 0.0))
            ch.add(pool.memset(head_row, 0.0))
            ch.add(pool.memset(head_of[:, :, :], 0.0))
            ch(pool.memset(own_seq[:, :], 1.0))
            n = 0
            for ins in [
                where(neg_tri[:, :], [[-1, P]], 0, 1, ALU.is_ge, 0.0),
                where(row0[:, :], [[0, P]], 0, -1, ALU.is_ge, 0.0),
                where(mask_att[:, 0:P], [[1, P]], -1, -1, ALU.is_ge, 0.0),
                where(mask_att[:, 2 * P:3 * P], [[1, P]], -1, -1, ALU.is_ge, 0.0),
                where(mask_ssm[:, 0:P], [[1, P]], 0, -1, ALU.is_ge, 0.0),
                where(mask_ssm[:, 2 * P:3 * P], [[1, P]], 0, -1, ALU.is_ge, 0.0),
                where(head_row, [[-1, SH], [0, P]], 0, 1, ALU.not_equal, 1.0),
                where(head_of[:, :, :].rearrange("h c (e p) -> h c e p", e=2),
                      [[-2, WC], [-1, 2], [0, DH]], 0, 1, ALU.not_equal, 1.0),
            ]:
                ch.add(ins)
            m4 = mask_new[:, :, :].rearrange("s b (h t) -> s b h t", h=H)
            seq_s = mask_ssms[:, :].rearrange("s (b t) -> s b t", b=NB)
            ch.add(where(m4, [[-NT, NB], [0, H], [0, NT]], 0, 1, ALU.is_ge, 0.0))
            ch.add(where(seq_s, [[-NT, NB], [0, NT]], 0, 1, ALU.is_ge, 0.0))
            ch.add(where(own_seq[:, :], [[-NT, NB]], 0, 1, ALU.is_ge, 0.0))
            ch.add(where(reset[:, 0:1], [[0, 1]], 0, 0, ALU.not_equal, 0.0))
            ch(where(reset[:, SEQ:T].rearrange("h (b t) -> h b t", b=NB), [[0, NB], [1, NT]], 0, 0,
                     ALU.not_equal, 0.0))
            ch.add(where(m4, [[NT, NB], [0, H], [1, NT]], -1, -1, ALU.is_ge, 0.0))
            ch.add(where(seq_s, [[NT, NB], [1, NT]], 0, -1, ALU.is_ge, 0.0))
            ch(where(own_seq[:, :], [[NT, NB]], NT - 1, -1, ALU.is_ge, 0.0))
            pool.sem_inc(s("masks"), 1)

            def store(dst, src):
                store.n += 1
                pool.dma_start(dst, src).then_inc(s("stored"), 16)
            store.n = 0

            def store_tokens(prompt, sample, tok):
                store(prompt.rearrange("(b p) n -> p b n", p=P), tok[:, 0:2, :])
                store(sample, tok[0:TS, 2, :])

            pool.wait_ge(s("k_tok_ready"), 3)
            store_tokens(o["k_prompt"][0, 0].rearrange("t h d -> t (h d)"),
                         o["k_sample"][0].rearrange("b t h d -> (b t) (h d)"), k_tok)
            pool.wait_ge(s("v_tok_ready"), 3)
            store_tokens(o["v_prompt"][0, 0].rearrange("t h d -> t (h d)"),
                         o["v_sample"][0].rearrange("b t h d -> (b t) (h d)"), v_tok)
            pool.wait_ge(s("xbc_tok_ready"), 2)
            store(o["ssm_conv_prompt"][0, 0], xbc_tok[P - TS - (KS - 1):P - TS, :])
            for b in range(NB):
                store(o["ssm_conv_sample"][0, b], xbc_tok[P - TS + NT * (b + 1) - (KS - 1):P - TS + NT * (b + 1), :])
            keep = KC - 1 - NT
            store(o["cf_conv_sample"][0][:, 0:keep, :], a["state_cf_conv"][0][:, NT:KC - 1, :])
            pool.wait_ge(s("u_tok_ready"), 2)
            store(o["cf_conv_prompt"][0, 0], u_tok[TS - (KC - 1):TS, 0, :])
            for b in range(NB):
                store(o["cf_conv_sample"][0, b, keep:KC - 1, :], u_tok[NT * b:NT * (b + 1), 1, :])
            pool.wait_ge(s("stored"), 16 * store.n)
            pool.sem_inc(s("slot2_stored"), 1)
            pool.wait_ge(s("prompt_state_ready"), 1)
            store(o["ssm_prompt"][0, 0].rearrange("(c e) p n -> (e p) c n", e=2), prompt_state)
            pool.wait_ge(s("states_new"), 2)
            store(o["ssm_sample"][0].rearrange("b (c e) p n -> (e p) b c n", e=2), states)
            pool.wait_ge(s("stored"), 16 * store.n)
            pool.sem_inc(s("slot3_stored"), 1)

            pool.wait_ge(s("merged"), 3 * DC)
            pool.memset(h_tok[TS:P, 2, :], 0.0).then_inc(s("h_tok_zero"), 1)
            pool.wait_ge(s("po_done"), H)
            ch(pool.memset(expert_row, 0.0))
            where(expert_row, [[-1, NE], [0, P]], 0, 1, ALU.not_equal, 1.0).then_inc(s("expert_row_ready"), 1)
            for i_, (t0, n) in enumerate(BLK):
                pool.wait_ge(s("y_low_ready"), i_ + 1)
                pool.wait_ge(s("y_high_ready"), i_ + 1)
                store(o["y_prompt"][0, t0:t0 + n, :] if i_ < 2 else o["y_sample"].rearrange("b t d -> (b t) d"),
                      y_tok[0:n, i_, :])
            pool.wait_ge(s("stored"), 16 * store.n)

        @block.scalar
        def _(act):
            ch = Chain(act, s("act_chain"))
            F = act.activation
            for r, name in ((MIX, "norm_mix"), (FFN, "norm_ffn"), (PLN, "norm_ple")):
                act.dma_start(raw_d[r:r + 1, :], a[name]).then_inc(s("par_loaded"), 16)
            act.dma_start(raw_d[FIN:FIN + 1, :], a["norm_final"].unsqueeze(0)).then_inc(s("par_loaded"), 16)
            act.dma_start(raw_d[CW:CW + KS, :], a["ssm_conv_w"][0]).then_inc(s("par_loaded"), 16)
            act.dma_start(raw_d[CB:CB + 1, :], a["ssm_conv_b"]).then_inc(s("par_loaded"), 16)
            act.dma_start(raw_d[CS:33, :], a["state_ssm_conv"][0].rearrange("b t c -> (b t) c")).then_inc(s("par_loaded"), 16)
            for r, name in ((SG, "ssm_norm"), (CFB, "cf_conv_b"), (LNG, "cf_ln_g"), (LNB, "cf_ln_b")):
                act.dma_start(raw_w[r:r + 1, :], a[name]).then_inc(s("par_loaded"), 16)
            act.dma_start(raw_w[CFW:CFW + KC, :], a["cf_conv_w"][0]).then_inc(s("par_loaded"), 16)
            act.dma_start(raw_cf, a["state_cf_conv"][0].rearrange("(a b) t c -> (b t) a c", a=2)).then_inc(s("par_loaded"), 16)
            act.dma_start(sb_bias, a["sb_bias"][0].unsqueeze(0).broadcast_to((P, H))).then_inc(s("small_loaded"), 16)
            for e in range(2):
                act.dma_start(d_skip[e * DH:(e + 1) * DH, :],
                              a["d_skip"][0].rearrange("(c e) -> e c", e=2)[e:e + 1, :].broadcast_to((DH, WC)),
                              allow_slow_non_contiguous=True).then_inc(s("small_loaded"), 16)
            act.dma_start(dt_bias, a["dt_bias"][0].unsqueeze(1)).then_inc(s("small_loaded"), 16)
            act.dma_start(a_log, a["a_log"][0].unsqueeze(1)).then_inc(s("small_loaded"), 16)
            act.dma_start(w_router[:, :, 0:NG], a["w_router_group"][0].rearrange("(k p) g -> p k g", p=P)).then_inc(s("small_loaded"), 16)
            act.dma_start(w_router[:, :, NG:NG + NE], a["w_router_expert"][0].rearrange("(k p) g e -> p k (g e)", p=P)).then_inc(s("small_loaded"), 16)

            act.dma_start(router_bias[:, 0:NG], a["b_router_group"].broadcast_to((P, NG))).then_inc(s("small_loaded"), 16)
            act.dma_start(router_bias[:, NG:NG + NE], a["b_router_expert"].rearrange("a g e -> a (g e)").broadcast_to((P, NE))
                          ).then_inc(s("small_loaded"), 16)
            act.dma_start(pages[:, :], a["page_table"].rearrange("(o b) p -> o (b p)", o=1)).then_inc(s("pages_loaded"), 16)

            def copy(out, in_):
                return F(out, in_, ACT.Copy)

            for c in range(DC):
                act.wait_ge(s("x_turned"), c + 1)
                copy(x[:, c, :], bank[c % 4][:, 0:T]).then_inc(s("x_ready"), 1)

            def norm_square(k):
                F(h[:, 0:DC // 2, :], x[:, 0:DC // 2, :], ACT.Square).then_inc(s("norm_squared"), 1)

            def norm_root(k, width):
                act.wait_ge(s("norm_summed"), k + 1)
                F(rows[:, 0, :], bank[7][:, 0:T], ACT.Sqrt, bias=eps[:, 0:1], scale=1.0 / width
                  ).then_inc(s("norm_rooted"), 1)

            act.wait_ge(s("x_ready"), DC)
            act.wait_ge(s("const"), 1)
            norm_square(0)
            norm_root(0, D)

            act.wait_ge(s("par_turned"), 3)
            copy(par_d[:, :, :], bank[4][:, 0:DC * 33].rearrange("p (c n) -> p c n", c=DC)).then_inc(s("par_ready"), 1)
            copy(par_w[:, :, :], bank[5][:, 0:WC * (4 + KC)].rearrange("p (c n) -> p c n", c=WC)).then_inc(s("par_ready"), 1)
            for c in range(WC):
                src = bank[6 - 2 * (c // 2)][:, 256 * (c % 2):256 * (c % 2) + 240] if c < 2 else \
                    bank[3][:, 256 * (c % 2):256 * (c % 2) + 240]
                copy(cpad_s[c][:, :, 0:KC - 1], src.rearrange("p (b t) -> p b t", b=NB)).then_inc(s("par_ready"), 1)

            act.sem_inc(s("proj_evac"), 4)
            with act.Fori(0, 4) as i:
                for t in range(8):
                    act.wait_ge(s("proj_done"), i * 8 + (t + 1))
                    copy(proj[:, bass.ds(i * 8 + t, 1), :].rearrange("p c t -> p (c t)"), bank[t % 4][:, 0:T]
                         ).then_inc(s("proj_evac"), 1)
            act.wait_ge(s("proj_evac"), 36)
            F(proj[:, TB:TB + WC, :], proj[:, TB:TB + WC, :], ACT.Sigmoid).then_inc(s("glu_sigmoid"), 1)

            def turned(name, out, b):
                act.wait_ge(s(name + "_turned"), turned.n.setdefault(name, 0) + 1)
                turned.n[name] += 1
                copy(out, b).then_inc(s(name + "_tok_ready"), 1)
            turned.n = {}
            for name, tok in (("k", k_tok), ("v", v_tok)):
                for i_, (t0, n) in enumerate(BLK):
                    turned(name, tok[0:n, i_, :], bank[5 + (i_ + (name == "v")) % 2][0:n, :])
            for i_ in range(2):
                turned("xbc", xbc_tok[:, 512 * i_:512 * (i_ + 1)], bank[5 + i_ % 2][:, :])

            with act.Fori(0, 3) as i:
                for t in range(8):
                    act.wait_ge(s("proj_done"), i * 8 + (32 + t + 1))
                    F(gates[:, bass.ds(i * 8 + t, 1), :].rearrange("p c t -> p (c t)"), bank[t % 4][:, 0:T],
                      ACT.Sigmoid).then_inc(s("proj_evac"), 1)

            act.wait_ge(s("u_turned"), 1)
            for g in range(2):
                copy(u_tok[:, g, :], bank[5 + g][0:TS, :]).then_inc(s("u_tok_ready"), 1)
            norm_root(1, W)
            for c in range(WC):
                act.wait_ge(s("ln_scaled"), 1)
                F(proj[:, TA + c, :], proj[:, TA + c, :], ACT.Silu, bias=par_w[:, c, LNB:LNB + 1],
                  scale=par_w[:, c, LNG:LNG + 1]).then_inc(s("cf_ready"), 1)
            act.wait_ge(s("xconv_done"), 1)
            F(proj[:, TX:TX + XCC, :], proj[:, TX:TX + XCC, :], ACT.Silu).then_inc(s("xconv_silu"), 1)
            F(proj[:, TZ:TZ + WC, :], proj[:, TZ:TZ + WC, :], ACT.Silu).then_inc(s("z_silu"), 1)
            act.wait_ge(s("cf_ready"), WC)
            act.wait_ge(s("small_loaded"), 16 * 9)
            act.wait_ge(s("dt_done"), 1)
            F(rows[0:SH, 0, :], bank[4][0:SH, 0:T], ACT.Identity, bias=dt_bias).then_inc(s("dt_raw"), 1)
            act.wait_ge(s("dt_raw"), 1)
            ch(F(rows[0:SH, 1, :], rows[0:SH, 0, :], ACT.Abs))
            ch(F(rows[0:SH, 1, :], rows[0:SH, 1, :], ACT.Exp, scale=-1.0))
            F(e_a, a_log, ACT.Exp).then_inc(s("dt_log"), 1)
            F(rows[0:SH, 1, :], rows[0:SH, 1, :], ACT.Ln, bias=1.0).then_inc(s("dt_log"), 1)
            act.wait_ge(s("decay_arg"), 2)
            F(rows[0:SH, 1, :], rows[0:SH, 1, :], ACT.Exp).then_inc(s("decay_exp"), 1)
            F(reset[:, 0:TS], rows[0:SH, 2, SEQ:T], ACT.Exp).then_inc(s("ecum_ready"), 1)
            for i_, (t0, n) in enumerate(BLK):
                act.wait_ge(s("b_turned"), max(i_ + 1, 2))
                copy(b_tok[0:n, i_, :], bank[3 + 3 * (i_ // 2)][0:n, 256 * (i_ % 2):256 * (i_ % 2) + 256]
                     ).then_inc(s("b_tok_ready"), 1)
            for hd in range(SH):
                act.wait_ge(s("seg_ready"), 3 * (hd + 1))
                F(seg[:, hd % 2, 0:3 * P], seg[:, hd % 2, 0:3 * P], ACT.Exp).then_inc(s("seg_exp"), 1)
                F(seg[0:TS, hd % 2, 3 * P:3 * P + TS], seg[0:TS, hd % 2, 3 * P:3 * P + TS], ACT.Exp
                  ).then_inc(s("seg_exp"), 1)
                act.wait_ge(s("y_done"), hd + 1)
                e = hd % 2
                copy(proj[e * DH:(e + 1) * DH, TB + hd // 2, :], bank[2 + hd % 2][e * DH:(e + 1) * DH, 0:T]
                     ).then_inc(s("y_ready"), 1)
            for b in range(NB):
                act.wait_ge(s("h0_turned"), b + 1)
                if b >= 2:
                    act.wait_ge(s("y_state_done"), b - 1)
                copy(h0_t[:, b % 2, :], bank[6 + b % 2][:, :]).then_inc(s("h0_ready"), 1)
            act.wait_ge(s("prompt_state_done"), 1)
            copy(prompt_state.rearrange("p c n -> p (c n)"), bank[5][:, :]).then_inc(s("prompt_state_ready"), 1)
            norm_root(2, W)

            def softplus_log(out, z, n, **bias):
                ch(F(out, z, ACT.Abs, **bias))
                ch(F(out, out, ACT.Exp, scale=-1.0))
                return F(out, out, ACT.Ln, bias=1.0)

            act.wait_ge(s("z_done"), 1)
            act.wait_ge(s("slot3_stored"), 1)
            softplus_log(w_new, bank[4][0:TS, :].rearrange("p (b n) -> p b n", b=NB), TS).then_inc(s("z_log"), 1)
            act.wait_ge(s("pw_arg"), 1)
            F(w_new, w_new, ACT.Exp).then_inc(s("pw_exp"), 1)
            act.sem_inc(s("even_copied"), 1)
            with act.Fori(0, NB // 2) as i:
                ch.begin(i, 4)
                for u in range(2):
                    for p in range(0, NPAGE, 2):
                        act.wait_ge(s("k_page_turned"), i * 16 + (8 * u + p + 1))
                        copy(k_turn[:, 0, :], bank[0][:, :]).then_inc(s("even_copied"), 1)
                    act.wait_ge(s("z_done"), i * 2 + (u + 2))
                    softplus_log(wgt[:, u, :], bank[2 + u][:, :], P).then_inc(s("z_log"), 1)
                for u in range(2):
                    act.wait_ge(s("c_done"), i * 2 + (u + 2))
                    F(wgt[:, u, :], bank[2 + u][:, :], ACT.Exp).then_inc(s("wgt_ready"), 1)
                ch.end(NB // 2)
            for hd in range(H):
                u, e, b_h = hd % 2, hd % 2, sb_bias[:, hd:hd + 1]
                act.wait_ge(s("z_done"), NB + 2 + hd)
                softplus_log(wgt[:, u, 0:3 * P], bank[u][:, 0:3 * P], P, bias=b_h).then_inc(s("z_log"), 1)
                act.wait_ge(s("pw_arg"), hd + 2)
                F(wgt[:, u, 0:3 * P], wgt[:, u, 0:3 * P], ACT.Exp).then_inc(s("pw_exp"), 1)
                act.wait_ge(s("po_done"), hd + 1)
                copy(att[e * DH:(e + 1) * DH, hd // 2, 0:SEQ], bank[2 + u][e * DH:(e + 1) * DH, 0:SEQ]
                     ).then_inc(s("att_ready"), 1)

            act.wait_ge(s("out_added"), DC)
            norm_square(3)
            norm_root(3, D)
            act.wait_ge(s("h_tok_zero"), 1)
            for n_ in range(6):
                n = BLK[n_ // 2][1]
                act.wait_ge(s("h_tok_turned"), n_ + 1)
                copy(h_tok[0:n, n_ // 2, 512 * (n_ % 2):512 * (n_ % 2) + 512], bank[4 + n_ % 4][0:n, :]
                     ).then_inc(s("h_tok_ready"), 1)
            act.wait_ge(s("router_arg"), 1)
            F(R["gexp"], R["gexp"], ACT.Exp).then_inc(s("router_exp"), 1)
            act.wait_ge(s("router_arg"), 2)
            F(R["w2"], R["w2"], ACT.Exp).then_inc(s("router_exp"), 1)
            act.wait_ge(s("comb_turned"), 1)
            copy(share_row, bank[3][0:NE, 0:T]).then_inc(s("share_row_ready"), 1)
            act.wait_ge(s("crowded_ready"), 1)
            with act.If(act.value_load(crowded[:, :], min_val=0, max_val=1) == 0):
                def h_low(e, u):
                    act.wait_ge(s("gathered_low"), e)
                    copy(h_exp[:, u, 0:512], bank[0][:, :]).then_inc(s("h_exp_low"), 1)

                def turn(i, last):
                    for e in range(4):
                        u, n = e % 2, i * 4 + (e + 1)
                        act.wait_ge(s("gate_done"), n)
                        F(silu_s, bank[3][:, :], ACT.Silu).then_inc(s("silu_ready"), 1)
                        act.wait_ge(s("weigh_turned"), n)
                        copy(weigh_s[:, u, :], bank[2][:, 0:T]).then_inc(s("share_ready"), 1)
                        if not (last and e == 3):
                            h_low(n + 1, 1 - u)
                        act.wait_ge(s("act_turned"), n)
                        copy(act_ft, bank[5][:, :]).then_inc(s("act_f_ready"), 1)
                        act.wait_ge(s("down_low"), n)
                        copy(y_exp[:, 0:512], bank[6][:, :]).then_inc(s("y_low"), 1)

                h_low(1, 0)
                with act.Fori(0, NE // 4 - 1) as i:
                    turn(i, False)
                turn(NE // 4 - 1, True)
            with act.Else():
                for e in range(NE):
                    act.wait_ge(s("spread_done"), e + 1)
                    copy(share[:, e, :], bank[4 + e % 4][:, 0:T]).then_inc(s("share_ready"), 1)
                with act.Fori(0, NE // 4) as i:
                    for t in range(16):
                        act.wait_ge(s("gate_done"), i * 16 + (t + 1))
                        F(silu_t[:, t % 4, :], bank[t % 4][:, 0:T], ACT.Silu).then_inc(s("silu_ready"), 1)

            act.wait_ge(s("moe_added"), 1)
            norm_square(4)
            norm_root(4, D)
            act.wait_ge(s("p_turned"), 1)
            for c in range(PLE // P):
                copy(p_feat[:, c, :], bank[4 + c][:, 0:T]).then_inc(s("p_ready"), 1)
            for m in range(DC):
                act.wait_ge(s("pg_done"), m + 1)
                if m >= 4:
                    act.wait_ge(s("pple_added"), m - 3)
                F(silu_t[:, m % 4, :], bank[m % 4][:, 0:T], ACT.Sigmoid).then_inc(s("pg_ready"), 1)
            act.wait_ge(s("pple_added"), DC)
            norm_square(5)
            norm_root(5, D)
            for i_, (t0, n) in enumerate(BLK):
                act.wait_ge(s("y_turned"), 2 * i_ + 1)
                copy(y_tok[0:n, i_, 0:512], bank[2 * i_][0:n, :]).then_inc(s("y_low_ready"), 1)

        @block.vector
        def _(dve):
            ch = Chain(dve, s("dve_chain"))
            TT, TSC, STT = dve.tensor_tensor, dve.tensor_scalar, dve.scalar_tensor_tensor

            def norm_square(k):
                TT(h[:, DC // 2:DC, :], x[:, DC // 2:DC, :], x[:, DC // 2:DC, :], ALU.mult
                   ).then_inc(s("norm_squared"), 1)

            def norm_inverse(k, width):
                r, v, t = rows[:, 0, :], rows[:, 1, :], rows[:, 2, :]
                dve.wait_ge(s("norm_rooted"), k + 1)
                ch.add(TSC(v, bank[7][:, 0:T], 1.0 / width, EPS, ALU.mult, ALU.add))
                ch(dve.reciprocal(r, r))
                ch(TT(t, r, r, ALU.mult))
                ch(TT(t, t, v, ALU.mult))
                ch(TSC(t, t, -0.5, 1.5, ALU.mult, ALU.add))
                ch(TT(r, r, t, ALU.mult))

            def norm_apply(col):
                for c in range(DC):
                    STT(h[:, c, :], x[:, c, :], par_d[:, c, col:col + 1], rows[:, 0, :], ALU.mult, ALU.mult
                        ).then_inc(s("h_ready"), 1)

            dve.wait_ge(s("x_ready"), DC)
            norm_square(0)
            norm_inverse(0, D)
            dve.wait_ge(s("par_ready"), 1)
            norm_apply(MIX)

            dve.wait_ge(s("proj_evac"), 4 + 24)
            dve.wait_ge(s("const"), 4)
            dve.wait_ge(s("par_ready"), 2 + WC)
            ch.add(TSC(proj[:, TQ:TQ + WC, :], proj[:, TQ:TQ + WC, :], float(DH) ** -0.5, None, ALU.mult))
            ch.add(dve.tensor_copy(xpad[:, :, KS - 1:XPAD], proj[:, TX:TX + XCC, 0:SEQ]))
            for c in range(XCC):
                ch.add(dve.tensor_copy(xpad_s[c][:, :, 0:KS - 1],
                                       par_d[:, c, CS:33].rearrange("p (b t) -> p b t", b=NB)))
                ch.add(dve.tensor_copy(xpad_s[c][:, :, KS - 1:],
                                       proj[:, TX + c, SEQ:T].rearrange("p (b t) -> p b t", b=NB)))
            ch.wait()
            dve.wait_ge(s("glu_sigmoid"), 1)
            TT(cpad[:, :, KC - 1:CPAD], proj[:, TA:TA + WC, 0:SEQ], proj[:, TB:TB + WC, 0:SEQ], ALU.mult
               ).then_inc(s("u_ready"), 1)
            ch(TT(proj[:, TB:TB + WC, SEQ:T], proj[:, TA:TA + WC, SEQ:T], proj[:, TB:TB + WC, SEQ:T], ALU.mult))
            for c in range(WC):
                dve.tensor_copy(cpad_s[c][:, :, KC - 1:], proj[:, TB + c, SEQ:T].rearrange("p (b t) -> p b t", b=NB)
                                ).then_inc(s("u_ready"), 1)
            dve.wait_ge(s("u_ready"), 1 + WC)

            def conv(tile, pad, pads, K, n, par, w0, bias):
                for k in range(K):
                    for c in range(n):
                        for out, src in ((proj[:, tile + c, 0:SEQ], pad[:, c, k:k + SEQ]),
                                         (proj[:, tile + c, SEQ:T].rearrange("p (b t) -> p b t", b=NB),
                                          pads[c][:, :, k:k + NT])):
                            w = par[:, c, w0 + k:w0 + k + 1]
                            if k == 0:
                                ch.add(TSC(out, src, w, par[:, c, bias:bias + 1], ALU.mult, ALU.add))
                            else:
                                ch.add(STT(out, src, w, out, ALU.mult, ALU.add))
                    ch.wait()

            conv(TA, cpad, cpad_s, KC, WC, par_w, CFW, CFB)
            dve.sem_inc(s("cconv_done"), 1)
            dve.wait_ge(s("xbc_turned"), 2)
            conv(TX, xpad, xpad_s, KS, XCC, par_d, CW, CB)
            dve.sem_inc(s("xconv_done"), 1)

            cf = proj[:, TA:TA + WC, :]
            dve.wait_ge(s("mean_summed"), 1)
            ch(TSC(rows[:, 1, :], bank[6][:, 0:T], 1.0 / W, None, ALU.mult))
            ch(TT(cf, cf, rows[:, 1:2, :].broadcast_to((P, WC, T)), ALU.subtract))
            dve.wait_ge(s("proj_done"), 56)
            TT(h[:, 0:WC, :], cf, cf, ALU.mult).then_inc(s("norm_squared"), 1)
            norm_inverse(1, W)
            TT(cf, cf, rows[:, 0:1, :].broadcast_to((P, WC, T)), ALU.mult).then_inc(s("ln_scaled"), 1)

            dve.wait_ge(s("masks"), 1)
            dve.wait_ge(s("small_loaded"), 16 * 9)
            dve.tensor_copy(bias_row[0:1, :, :].rearrange("p a (h t) -> p a h t", h=H),
                            sb_bias[0:1, :].unsqueeze(1).unsqueeze(3).broadcast_to((1, NPAGE, H, NT))
                            ).then_inc(s("bias_row_ready"), 1)

            dt, dec, cum = (rows[0:SH, j, :] for j in range(3))
            dve.wait_ge(s("dt_raw"), 1)
            dve.wait_ge(s("dt_log"), 2)
            dve.wait_ge(s("masks"), 1)
            ch(STT(dt, dt, 0.0, dec, ALU.max, ALU.add))
            ch(TSC(dec, dt, e_a, -1.0, ALU.mult, ALU.mult))
            ch(dve.tensor_tensor_scan(cum, reset[:, :], dec, 0.0, ALU.mult, ALU.add))
            TSC(dec[:, 0:SEQ], cum[:, 0:SEQ], -1.0, cum[:, SEQ - 1:SEQ], ALU.mult, ALU.add
                ).then_inc(s("decay_arg"), 1)
            cum_s = cum[:, SEQ:T].rearrange("h (b t) -> h b t", b=NB)
            TT(dec[:, SEQ:T].rearrange("h (b t) -> h b t", b=NB), cum_s[:, :, NT - 1:NT].broadcast_to((SH, NB, NT)), cum_s,
               ALU.subtract).then_inc(s("decay_arg"), 1)
            dve.wait_ge(s("decay_exp"), 1)
            TT(dec, dec, dt, ALU.mult).then_inc(s("rows_ready"), 1)
            dve.wait_ge(s("rows_turned"), 1)
            for i_, (n, b0, nb) in enumerate(((P, 0, 2), (TS, 2, 1))):
                src = bank[5][0:n, 24 * b0:24 * (b0 + nb)].rearrange("p (b k) -> p b k", b=nb)
                ch.add(dve.tensor_copy(tokp[0:n, b0:b0 + nb, 0:16], src[:, :, 0:16]))
                ch.add(TSC(tokp[0:n, b0:b0 + nb, 16:24], src[:, :, 16:24], -1.0, None, ALU.mult))
            ch.wait()
            dve.sem_inc(s("tokp_ready"), 1)
            for i_, (t0, n) in enumerate(BLK):
                dve.wait_ge(s("xs_turned"), i_ + 1)
                for j, out in enumerate((xdt, xdec)):
                    TT(out[0:n, i_, :].rearrange("p (h d) -> p h d", h=SH),
                       bank[i_][0:n, :].rearrange("p (h d) -> p h d", h=SH),
                       tokp[0:n, i_, 8 * j:8 * j + 8].unsqueeze(2).broadcast_to((n, SH, SP_)), ALU.mult
                       ).then_inc(s("xdt_ready"), 1)
            for g in range(2):
                dve.wait_ge(s("cb_done"), g + 1)
                b_ = bank[4 + 3 * g]
                TT(cb[:, g, 0:3 * P], b_[:, 0:3 * P], mask_ssm[:, :], ALU.mult).then_inc(s("cb_ready"), 1)
                TT(cb[0:TS, g, 3 * P:3 * P + TS], b_[0:TS, 3 * P:3 * P + TS], mask_ssms[:, :], ALU.mult
                   ).then_inc(s("cb_ready"), 1)
            dve.wait_ge(s("ecum_spread"), 1)
            dve.tensor_copy(ecum[:, :, :], bank[5][:, 256:512].rearrange("p (c t) -> p c t", c=WC)
                            ).then_inc(s("ecum_copied"), 1)
            for hd in range(SH):
                dve.wait_ge(s("cum_spread"), hd + 1)
                if hd >= 2:
                    dve.wait_ge(s("y_done"), hd - 1)
                b_, sg = bank[hd % 2], seg[:, hd % 2, :]
                for (n, o_, w, i_, t0) in ((P, 0, 2 * P, 0, 0), (P, 2 * P, P, 1, P), (TS, 3 * P, TS, 2, 2 * P)):
                    TSC(sg[0:n, o_:o_ + w], b_[0:n, t0:t0 + w], tokp[0:n, i_, 16 + hd:17 + hd], 0.0,
                        ALU.add, ALU.min).then_inc(s("seg_ready"), 1)
                dve.wait_ge(s("seg_exp"), 2 * (hd + 1))
                g = hd // (SH // 2)
                TT(sg[:, 0:3 * P], sg[:, 0:3 * P], cb[:, g, 0:3 * P], ALU.mult).then_inc(s("w_ready"), 1)
                TT(sg[0:TS, 3 * P:3 * P + TS], sg[0:TS, 3 * P:3 * P + TS], cb[0:TS, g, 3 * P:3 * P + TS],
                   ALU.mult).then_inc(s("w_ready"), 1)
            y = proj[:, TB:TB + WC, :]
            dve.wait_ge(s("y_state_done"), NB)
            dve.wait_ge(s("ecum_copied"), 1)
            dve.wait_ge(s("y_ready"), SH)
            dve.wait_ge(s("h0_ready"), NB)
            ys = h0_t[:, 0, 0:256].rearrange("p (c t) -> p c t", c=WC)
            ch(TT(ys, bank[4][:, 0:256].rearrange("p (c t) -> p c t", c=WC), ecum[:, :, :], ALU.mult))
            ch(TT(y[:, :, SEQ:T], y[:, :, SEQ:T], ys, ALU.add))
            for c in range(WC):
                ch.add(STT(y[:, c, :], proj[:, TX + c, :], d_skip[:, c:c + 1], y[:, c, :], ALU.mult, ALU.add))
            ch.wait()
            dve.wait_ge(s("z_silu"), 1)
            ch(TT(y, y, proj[:, TZ:TZ + WC, :], ALU.mult))
            dve.wait_ge(s("b_tok_ready"), 3)
            for q in range(2):
                if q:
                    dve.wait_ge(s("new_state_done"), WC)
                for b in range(4):
                    TSC(b_own[:, b, :], b_tok[0:TS, 2, :], own_seq[:, 4 * q + b:4 * q + b + 1], None, ALU.mult
                        ).then_inc(s("b_own_ready"), 1)
                for c in range(WC):
                    dve.wait_ge(s("new_state_done"), WC * q + c + 1)
                    for b in range(4):
                        st = states[:, 4 * q + b, c, :]
                        tl = NT * (4 * q + b) + NT - 1
                        ch.add(STT(st, st, ecum[:, c, tl:tl + 1], bank[c][:, P * b:P * (b + 1)], ALU.mult, ALU.add))
                ch.wait()
                dve.sem_inc(s("states_new"), 1)
            dve.wait_ge(s("y_done"), SH)
            dve.wait_ge(s("prompt_state_done"), 1)
            TT(xdt_sq, y, y, ALU.mult).then_inc(s("norm_squared"), 1)
            norm_inverse(2, W)
            for c in range(WC):
                STT(y[:, c, :], y[:, c, :], par_w[:, c, SG:SG + 1], rows[:, 0, :], ALU.mult, ALU.mult
                    ).then_inc(s("ssm_ready"), 1)

            ch(dve.memset(scratch[:, 0:2560], 0.0))
            for e in range(2):
                hf = slice(e * DH, (e + 1) * DH)
                dve.tensor_copy(q_pair[hf, :, :, NT * e:NT * (e + 1)].rearrange("p b c t -> p c b t"),
                                proj[hf, TQ:TQ + WC, SEQ:T].rearrange("p c (b t) -> p c b t", b=NB)
                                ).then_inc(s("q_spread"), 1)
                dve.tensor_copy(q_head[hf, e:H:2, :], proj[hf, TQ:TQ + WC, 0:SEQ]).then_inc(s("q_spread"), 1)
            for u in range(2):
                dve.memset(later[:, u, 448:512], 0.0).then_inc(s("later_zero"), 1)
            dve.wait_ge(s("later_zero"), 2)
            dve.wait_ge(s("z_log"), 1)
            zn = bank[4][0:TS, :].rearrange("p (b n) -> p b n", b=NB)
            ch(STT(soft_new, zn, 0.0, w_new, ALU.max, ALU.add))
            TT(soft_new, soft_new, mask_new[:, :, :], ALU.mult).then_inc(s("soft_new"), 1)
            dve.wait_ge(s("c_done"), 1)
            TSC(w_new, zn, 0.0, None, ALU.min).then_inc(s("pw_arg"), 1)
            dve.wait_ge(s("pw_exp"), 1)
            TT(w_new, w_new, mask_new[:, :, :], ALU.mult).then_inc(s("w_new"), 1)
            dve.wait_ge(s("soft_new"), 1)
            dve.sem_inc(s("odd_copied"), 1)
            dve.sem_inc(s("o_copied"), 4)
            with dve.Fori(0, NB // 2) as i:
                ch.begin(i, 2 * (NPAGE - 1))
                for u in range(2):
                    for p in range(1, NPAGE, 2):
                        dve.wait_ge(s("k_page_turned"), i * 16 + (8 * u + p + 1))
                        dve.tensor_copy(k_turn[:, 1, :], bank[1][:, :]).then_inc(s("odd_copied"), 1)
                    dve.wait_ge(s("z_log"), i * 2 + (u + 2))
                    ch.add(STT(soft[:, u, :], bank[2 + u][:, :], 0.0, wgt[:, u, :], ALU.max, ALU.add))
                    dve.tensor_copy(later[0:TS, u, 448:512],
                                    soft_new[:, bass.ds(i * 2 + u, 1), :].rearrange("p b n -> p (b n)")
                                    ).then_inc(s("soft_ready"), 1)
                    dve.wait_ge(s("soft_ready"), i * 4 + (2 * u + 1))
                    ch.wait()
                    for p in range(NPAGE - 2, -1, -1):
                        lt, nx = later[:, u, 64 * p:64 * (p + 1)], slice(64 * (p + 1), 64 * (p + 2))
                        ins = TT(lt, later[:, u, nx], soft[:, u, nx], ALU.add)
                        if p:
                            ch(ins)
                        else:
                            ins.then_inc(s("soft_ready"), 1)
                for u in range(2):
                    dve.wait_ge(s("o_done"), i * 2 + (u + 1))
                    for e in range(2):
                        hf = slice(e * DH, (e + 1) * DH)
                        ins = dve.tensor_copy(att[hf, :, bass.ds(i * (2 * NT) + (SEQ + NT * u), NT)],
                                              bank[5 + u][hf, 0:64].rearrange("p (c k) -> p c k", c=WC)[:, :, NT * e:NT * (e + 1)])
                        ins.then_inc(s("o_copied"), 1)
                ch.end(NB // 2)
            for hd in range(H):
                u, b_h = hd % 2, sb_bias[:, hd:hd + 1]
                sf, wg, z = soft[:, u, 0:3 * P], wgt[:, u, 0:3 * P], bank[u][:, 0:3 * P]
                dve.wait_ge(s("z_log"), NB + 2 + hd)
                ch(TSC(sf, z, b_h, 0.0, ALU.add, ALU.max))
                ch(TT(sf, sf, wg, ALU.add))
                TT(sf, sf, mask_att[:, :], ALU.mult).then_inc(s("p_soft"), 1)
                dve.wait_ge(s("c_done"), NB + 2 + hd)
                TSC(wg, z, b_h, 0.0, ALU.add, ALU.min).then_inc(s("pw_arg"), 1)
                dve.wait_ge(s("pw_exp"), hd + 2)
                TT(wg, wg, mask_att[:, :], ALU.mult).then_inc(s("pw_ready"), 1)

            n_ = 0
            for j, n in enumerate((1, 2, 0)):
                for m in range(DC):
                    dve.wait_ge(s("branch_done"), n_ + 1)
                    b_, g_ = bank[4 + n_ % 4][:, 0:T], gates[:, n * DC + m, :]
                    if j == 0:
                        TT(merged[:, m, :], b_, g_, ALU.mult).then_inc(s("merged"), 1)
                    else:
                        ch(TT(g_, b_, g_, ALU.mult))
                        dve.wait_ge(s("merged"), n_ - 7)
                        TT(merged[:, m, :], merged[:, m, :], g_, ALU.add).then_inc(s("merged"), 1)
                    n_ += 1
            for m in range(DC):
                dve.wait_ge(s("out_done"), m + 1)
                TT(x[:, m, :], x[:, m, :], bank[m % 4][:, 0:T], ALU.add).then_inc(s("out_added"), 1)

            dve.wait_ge(s("out_added"), DC)
            norm_square(3)
            norm_inverse(3, D)
            norm_apply(FFN)
            dve.wait_ge(s("h_ready"), 2 * DC)
            ch(dve.memset(R["logit"], 0.0))
            for i_, (t0, n) in enumerate(BLK):
                dve.wait_ge(s("logits_done"), i_ + 1)
                ch(TT(R["logit"][0:n, i_, :], bank[i_][0:n, 0:NG + NE], router_bias[0:n, :], ALU.add))
            gl, el = R["logit"][:, :, 0:NG], R["logit"][:, :, NG:NG + NE]

            def wide(t, n):
                return t.broadcast_to((P, 3, n))

            def first_max(out, v, top, pri, one):
                ch(dve.tensor_reduce(top, v, AX.X, ALU.max))
                ch(TT(out, v, wide(top, EG), ALU.is_equal))
                ch(TT(pri, out, descend.unsqueeze(1).broadcast_to((P, 3, EG)), ALU.mult))
                ch(dve.tensor_reduce(one, pri, AX.X, ALU.max))
                ch(TT(out, pri, wide(one, EG), ALU.is_equal))

            first_max(R["goh"], gl, R["gmax"], R["gpri"], R["gone"])
            TT(R["gexp"], gl, wide(R["gmax"], NG), ALU.subtract).then_inc(s("router_arg"), 1)
            ch(TT(R["pick"].rearrange("p b (g e) -> p b g e", g=NG), el.rearrange("p b (g e) -> p b g e", g=NG),
                  R["goh"].unsqueeze(3).broadcast_to((P, 3, NG, EG)), ALU.mult))
            ch(dve.tensor_reduce(R["esel"], R["pick"].rearrange("p b (g e) -> p b e g", g=NG), AX.X, ALU.add))
            first_max(R["o1"], R["esel"], R["m1"], R["pri"], R["one"])
            ch(STT(R["esel2"], R["o1"], -1e30, R["esel"], ALU.mult, ALU.add))
            first_max(R["o2"], R["esel2"], R["m2"], R["pri"], R["one"])
            TT(R["w2"], R["m2"], R["m1"], ALU.subtract).then_inc(s("router_arg"), 1)
            dve.wait_ge(s("router_exp"), 1)
            ch(dve.tensor_reduce(R["gsum"], R["gexp"], AX.X, ALU.add))
            dve.wait_ge(s("router_exp"), 2)
            ch(TSC(R["den"], R["w2"], 1.0, None, ALU.add))
            ch(TT(R["den"], R["den"], R["gsum"], ALU.mult))
            ch(dve.reciprocal(R["w1"], R["den"]))
            ch(TT(R["w2"], R["w2"], R["w1"], ALU.mult))
            ch(TT(R["o1"], R["o1"], wide(R["w1"], EG), ALU.mult))
            ch(TT(R["o2"], R["o2"], wide(R["w2"], EG), ALU.mult))
            ch(TT(R["comb4"], R["o1"], R["o2"], ALU.add))
            TT(R["comb"].rearrange("p b (g e) -> p b g e", g=NG), R["goh"].unsqueeze(3).broadcast_to((P, 3, NG, EG)),
               R["comb4"].unsqueeze(2).broadcast_to((P, 3, NG, EG)), ALU.mult).then_inc(s("comb_ready"), 1)

            dve.wait_ge(s("share_row_ready"), 1)
            ch.add(TSC(taken, share_row, 0.0, None, ALU.is_gt))
            ch.add(dve.memset(one_row, 1.0))
            ch.add(dve.tensor_tensor_scan(count_to[:, :], ones[:, :], ones[:, :], 0.0, ALU.mult, ALU.add))
            ch(dve.memset(slot_no, 0.0))
            ch(dve.tensor_tensor_scan(rank, one_row, taken, 0.0, ALU.mult, ALU.add))
            TT(taken, taken, rank, ALU.mult).then_inc(s("slots_ready"), 1)
            dve.wait_ge(s("slots_turned"), 1)
            ch(dve.tensor_reduce(most, bank[3][0:1, 64:64 + NE], AX.X, ALU.max))
            TSC(crowded[:, :], most, CAP + 0.5, None, ALU.is_gt).then_inc(s("crowded_ready"), 1)
            ch.add(dve.tensor_copy(slot_no[:, 0:2, :], bank[3][:, 0:2 * NE].rearrange("p (b e) -> p b e", b=2)))
            ch(dve.tensor_copy(slot_no[0:TS, 2, :], bank[3][0:TS, 2 * NE:3 * NE]))
            dve.wait_ge(s("crowded_ready"), 1)
            with dve.If(dve.value_load(crowded[:, :], min_val=0, max_val=1) == 0):
                def pick(e, u):
                    shape = (P, 3, P)
                    TT(pick_t[:, u, :, :], count_to[:, :].unsqueeze(1).broadcast_to(shape),
                       slot_no[:, :, bass.ds(e, 1)].broadcast_to(shape), ALU.is_equal).then_inc(s("pick_ready"), 1)
                    dve.wait_ge(s("pick_ready"), e + 1)
                    TT(weigh_t[:, u, :, :], pick_t[:, u, :, :], R["comb"][:, :, bass.ds(e, 1)].broadcast_to(shape),
                       ALU.mult).then_inc(s("weigh_ready"), 1)

                def h_high(e, u):
                    dve.wait_ge(s("gathered_high"), e)
                    dve.tensor_copy(h_exp[:, u, 512:1024], bank[1][:, :]).then_inc(s("h_exp_high"), 1)

                def add(e):
                    for c in range(DC):
                        dve.wait_ge(s("spread_done"), e * 8 + (c - 7))
                        TT(x[:, c, :], x[:, c, :], bank[(6, 7, 3, 4)[c % 4]][:, 0:T], ALU.add).then_inc(s("down_added"), 1)

                def turn(i, first, last):
                    for e in range(4):
                        u, n = e % 2, i * 4 + (e + 1)
                        later_ = not (first and e == 0)
                        if not (last and e == 3):
                            if later_:
                                dve.wait_ge(s("gathered_high"), n + (-1))
                                dve.wait_ge(s("weigh_turned"), n + (-1))
                            pick(n, 1 - u)
                        dve.wait_ge(s("up_done"), n)
                        dve.wait_ge(s("silu_ready"), n)
                        if later_:
                            dve.wait_ge(s("act_turned"), n + (-1))
                        TT(act_s, bank[4][:, :], silu_s, ALU.mult).then_inc(s("act_ready"), 1)
                        if not (last and e == 3):
                            h_high(n + 1, 1 - u)
                        if later_:
                            add(n + (-1))
                        dve.wait_ge(s("down_done"), n)
                        dve.tensor_copy(y_exp[:, 512:1024], bank[7][:, :]).then_inc(s("y_high"), 1)

                pick(0, 0)
                h_high(1, 0)
                turn(0, True, False)
                with dve.Fori(1, NE // 4 - 1) as i:
                    turn(i, False, False)
                turn(NE // 4 - 1, False, True)
                add(NE)
                dve.wait_ge(s("down_added"), DC * NE)
                dve.sem_inc(s("moe_added"), 1)
            with dve.Else():
                ch_e = Chain(dve, s("pick_ready"))
                dve.wait_ge(s("share_ready"), NE)
                dve.sem_inc(s("down_added"), 8)
                with dve.Fori(0, NE // 4) as i:
                    ch_e.begin(i, 16)
                    for e in range(4):
                        for m in range(4):
                            t = 4 * e + m
                            dve.wait_ge(s("up_done"), i * 16 + (t + 1))
                            dve.wait_ge(s("silu_ready"), i * 16 + (t + 1))
                            ch_e(TT(act_t[:, m, :], bank[4 + m][:, 0:T],
                                  share[:, bass.ds(i * 4 + e, 1), :].rearrange("p e t -> p (e t)"), ALU.mult))
                            TT(act_t[:, m, :], act_t[:, m, :], silu_t[:, m, :], ALU.mult).then_inc(s("act_ready"), 1)
                        for m in range(DC):
                            dve.wait_ge(s("down_done"), i * 32 + (8 * e + m + 1))
                            TT(x[:, m, :], x[:, m, :], bank[m % 4][:, 0:T], ALU.add).then_inc(s("down_added"), 1)
                    ch_e.end(NE // 4)
                dve.wait_ge(s("down_added"), 8 + DC * NE)
                dve.sem_inc(s("moe_added"), 1)

            norm_square(4)
            norm_inverse(4, D)
            norm_apply(PLN)
            for m in range(DC):
                dve.wait_ge(s("pg_ready"), m + 1)
                dve.wait_ge(s("pp_done"), m + 1)
                ch(TT(silu_t[:, m % 4, :], bank[4 + m % 4][:, 0:T], silu_t[:, m % 4, :], ALU.mult))
                TT(x[:, m, :], x[:, m, :], silu_t[:, m % 4, :], ALU.add).then_inc(s("pple_added"), 1)
            dve.wait_ge(s("pple_added"), DC)
            norm_square(5)
            norm_inverse(5, D)
            norm_apply(FIN)
            for i_, (t0, n) in enumerate(BLK):
                dve.wait_ge(s("y_turned"), 2 * i_ + 2)
                dve.tensor_copy(y_tok[0:n, i_, 512:1024], bank[2 * i_ + 1][0:n, :]).then_inc(s("y_high_ready"), 1)

        @block.tensor
        def _(pe):
            MM, TR = pe.matmul, pe.transpose

            pe.wait_ge(s("ident_ready"), 1)
            pe.wait_ge(s("x_loaded"), 32)
            for c in range(DC):
                if c >= 4:
                    pe.wait_ge(s("x_ready"), c - 3)
                for i_, (t0, n) in enumerate(BLK):
                    m = TR(bank[c % 4][:, t0:t0 + n], x_tok[0:n, i_, c * P:(c + 1) * P], ident[0:n, 0:n])
                m.then_inc(s("x_turned"), 1)
            pe.wait_ge(s("par_loaded"), 13 * 16)
            for c in range(DC):
                m = TR(bank[4][:, 33 * c:33 * (c + 1)], raw_d[:, c * P:(c + 1) * P], ident[0:33, 0:33])
            m.then_inc(s("par_turned"), 1)
            n = 4 + KC
            for c in range(WC):
                m = TR(bank[5][:, n * c:n * (c + 1)], raw_w[:, c * P:(c + 1) * P], ident[0:n, 0:n])
            m.then_inc(s("par_turned"), 1)
            pe.wait_ge(s("x_ready"), DC)
            for c in range(WC):
                b_ = bank[6] if c < 2 else bank[3]
                for q in range(2):
                    t0 = 256 * (c % 2) + 120 * q
                    m = TR(b_[:, t0:t0 + 120], raw_cf[:, q, c * P:(c + 1) * P], ident[0:120, 0:120])
            m.then_inc(s("par_turned"), 1)

            def norm_sum(k, src, n):
                for c in range(n):
                    m = MM(bank[7][:, 0:T], ones[:, :], src[:, c, :], start=c == 0, stop=c == n - 1)
                m.then_inc(s("norm_summed"), 1)

            pe.wait_ge(s("const"), 2)
            pe.wait_ge(s("norm_squared"), 2)
            norm_sum(0, h, DC)

            pe.wait_ge(s("par_ready"), 2 + WC)
            pe.wait_ge(s("w_dt_loaded"), 16)
            for k in range(DC):
                pe.wait_ge(s("h_ready"), k + 1)
                m = MM(bank[4][0:SH, 0:T], w_dt[:, k, :], h[:, k, :], start=k == 0, stop=k == DC - 1)
            m.then_inc(s("dt_done"), 1)

            def project(i, first):
                for j in range(2):
                    pe.wait_ge(s(f"w_in_loaded{j}"), i * 16 + (first // 8 * 16 + 16))
                    for t in range(4 * j, 4 * j + 4):
                        pe.wait_ge(s("proj_evac"), i * 8 + (first + t + 1))
                        for k in range(DC):
                            m = MM(bank[t % 4][:, 0:T], slot(j, DC, GROUP)[:, k, (t % 4) * P:(t % 4 + 1) * P],
                                   h[:, k, :], start=k == 0, stop=k == DC - 1)
                        m.then_inc(s("proj_done"), 1)

            with pe.Fori(0, 4) as i:
                project(i, 0)

            def turn(name, b_, src, t0, n, chunks):
                for c in range(chunks):
                    m = TR(b_[0:n, c * P:(c + 1) * P], src(c)[:, t0:t0 + n], ident[:, :])
                m.then_inc(s(name + "_turned"), 1)

            pe.wait_ge(s("proj_evac"), 4 + 32)
            pe.wait_ge(s("x_ready"), DC)
            n_ = 0
            for name, tile in (("k", TK), ("v", TV)):
                for i_, (t0, n) in enumerate(BLK):
                    if n_ >= 2:
                        if n_ - 2 < 3:
                            pe.wait_ge(s("k_tok_ready"), n_ - 1)
                        else:
                            pe.wait_ge(s("v_tok_ready"), n_ - 4)
                    turn(name, bank[5 + n_ % 2], lambda c: proj[:, tile + c, :], t0, n, WC)
                    n_ += 1
            for q in range(2):
                pe.wait_ge(s("v_tok_ready"), 2 + q)
                turn("xbc", bank[5 + q], lambda c: proj[:, TX + 4 * q + c, :], T - P, P, WC)

            with pe.Fori(0, 3) as i:
                project(i, 32)

            pe.wait_ge(s("u_ready"), 1 + WC)
            pe.wait_ge(s("xbc_tok_ready"), 2)
            for c in range(WC):
                TR(bank[5][0:TS, c * P:(c + 1) * P], cpad[:, c, CPAD - TS:CPAD], ident[:, :])
            for c in range(WC):
                m = TR(bank[6][0:TS, c * P:(c + 1) * P], proj[:, TB + c, SEQ:T], ident[:, :])
            m.then_inc(s("u_turned"), 1)
            pe.wait_ge(s("u_tok_ready"), 2)
            pe.wait_ge(s("cconv_done"), 1)
            for c in range(WC):
                m = MM(bank[6][:, 0:T], ones[:, :], proj[:, TA + c, :], start=c == 0, stop=c == WC - 1)
            m.then_inc(s("mean_summed"), 1)
            pe.wait_ge(s("norm_squared"), 3)
            norm_sum(1, h, WC)

            pe.wait_ge(s("rows_ready"), 1)
            pe.wait_ge(s("decay_exp"), 1)
            for i_, (t0, n) in enumerate(BLK):
                for j, r in enumerate((0, 1, 2)):
                    m = TR(bank[5][0:n, 24 * i_ + 8 * j:24 * i_ + 8 * j + 8], rows[0:SH, r, t0:t0 + n],
                           ident[0:SH, 0:SH])
            m.then_inc(s("rows_turned"), 1)
            pe.wait_ge(s("ecum_ready"), 1)
            pe.wait_ge(s("tokp_ready"), 1)
            for c in range(WC):
                m = MM(bank[5][:, 256 + TS * c:256 + TS * (c + 1)], head_of[:, c, :], reset[:, 0:TS], start=True, stop=True)
            m.then_inc(s("ecum_spread"), 1)
            pe.wait_ge(s("xconv_silu"), 1)
            pe.wait_ge(s("proj_evac"), 60)
            for i_, (t0, n) in enumerate(BLK):
                turn("xs", bank[i_], lambda c: proj[:, TX + c, :], t0, n, WC)
            TBB, TCC = TX + WC, TX + WC + 2
            for i_, (t0, n) in enumerate(BLK):
                b0 = 256 * (i_ % 2)
                for g in range(2):
                    m = TR(bank[3 + 3 * (i_ // 2)][0:n, b0 + P * g:b0 + P * (g + 1)], proj[:, TBB + g, t0:t0 + n], ident[:, :])
                m.then_inc(s("b_turned"), 1)
            pe.wait_ge(s("ln_scaled"), 1)
            for g in range(2):
                b_, B_, C_ = bank[4 + 3 * g], proj[:, TBB + g, :], proj[:, TCC + g, :]
                MM(b_[:, 0:2 * P], B_[:, 0:P], C_[:, 0:SEQ], start=True, stop=True)
                MM(b_[:, 2 * P:3 * P], B_[:, P:SEQ], C_[:, P:SEQ], start=True, stop=True)
                MM(b_[0:TS, 3 * P:3 * P + TS], B_[:, SEQ:T], C_[:, SEQ:T], start=True, stop=True
                   ).then_inc(s("cb_done"), 1)

            def spread_cum(hd):
                MM(bank[hd % 2][:, 0:T], head_row[:, hd, :], rows[0:SH, 2, :], start=True, stop=True
                   ).then_inc(s("cum_spread"), 1)

            pe.wait_ge(s("xdt_ready"), 6)
            pe.wait_ge(s("b_tok_ready"), 3)
            spread_cum(0)
            spread_cum(1)
            for hd in range(SH):
                c = hd // 2
                pe.wait_ge(s("w_ready"), 2 * (hd + 1))
                if hd >= 2:
                    pe.wait_ge(s("y_ready"), hd - 1)
                b_, sg = bank[2 + hd % 2], seg[:, hd % 2, :]
                MM(b_[:, 0:SEQ], xdt[:, 0, c * P:(c + 1) * P], sg[:, 0:SEQ], start=True, stop=False)
                MM(b_[:, P:SEQ], xdt[:, 1, c * P:(c + 1) * P], sg[:, SEQ:SEQ + P], start=False, stop=True)
                MM(b_[:, SEQ:T], xdt[0:TS, 2, c * P:(c + 1) * P], sg[0:TS, 3 * P:3 * P + TS], start=True, stop=True
                   ).then_inc(s("y_done"), 1)
                if hd + 2 < SH:
                    spread_cum(hd + 2)
            pe.wait_ge(s("states_loaded"), 16)
            pe.wait_ge(s("cb_ready"), 4)

            def turn_state(b):
                if b >= 2:
                    pe.wait_ge(s("h0_ready"), b - 1)
                for c in range(WC):
                    m = TR(bank[6 + b % 2][:, c * P:(c + 1) * P], states[:, b, c, :], ident[:, :])
                m.then_inc(s("h0_turned"), 1)

            turn_state(0)
            for b in range(NB):
                if b + 1 < NB:
                    turn_state(b + 1)
                pe.wait_ge(s("h0_ready"), b + 1)
                for c in range(WC):
                    m = MM(bank[4][:, TS * c + NT * b:TS * c + NT * (b + 1)], h0_t[:, b % 2, c * P:(c + 1) * P],
                           proj[:, TCC + c // 2, SEQ + NT * b:SEQ + NT * (b + 1)], start=True, stop=True)
                m.then_inc(s("y_state_done"), 1)
            pe.wait_ge(s("ecum_copied"), 1)
            for c in range(WC):
                for i_ in range(2):
                    m = MM(bank[5][:, c * P:(c + 1) * P], xdec[:, i_, c * P:(c + 1) * P],
                           b_tok[:, i_, (c // 2) * P:(c // 2 + 1) * P], start=i_ == 0, stop=i_ == 1)
            m.then_inc(s("prompt_state_done"), 1)
            pe.wait_ge(s("y_ready"), SH)
            for q in range(2):
                pe.wait_ge(s("b_own_ready"), 4 * (q + 1))
                for c in range(WC):
                    MM(bank[c][:, :], xdec[0:TS, 2, c * P:(c + 1) * P], b_own[:, :, (c // 2) * P:(c // 2 + 1) * P],
                       start=True, stop=True).then_inc(s("new_state_done"), 1)
            pe.wait_ge(s("norm_squared"), 4)
            norm_sum(2, xdt_sq, WC)

            pe.wait_ge(s("states_new"), 2)
            pe.wait_ge(s("prompt_state_ready"), 1)
            pe.wait_ge(s("ssm_ready"), WC)
            pe.wait_ge(s("q_spread"), 4)
            pe.wait_ge(s("bias_row_ready"), 1)
            pe.wait_ge(s("masks"), 1)
            bias2 = bias_row[:, :, :].rearrange("p a n -> p (a n)")
            MM(bank[4][0:TS, :], row0[:, 0:TS], bias2, start=True, stop=False)
            for c in range(WC):
                m = MM(bank[4][0:TS, :].rearrange("p (b n) -> p b n", b=NB)[:, :, 16 * c:16 * (c + 1)],
                       proj[:, TK + c, SEQ:T], q_pair[:, :, c, :], start=False, stop=c == WC - 1)
            m.then_inc(s("z_done"), 1)
            pe.wait_ge(s("soft_new"), 1)
            MM(bank[4][0:TS, :], neg_tri[0:TS, 0:TS], soft_new.rearrange("p b n -> p (b n)"), start=False, stop=True,
               skip_group_check=True).then_inc(s("c_done"), 1)
            pe.wait_ge(s("w_new"), 1)

            with pe.Fori(0, NB // 2) as i:
                for u in range(2):
                    kp = slot((2, 0)[u], NPAGE, W)
                    copied = (s("even_copied"), s("odd_copied"))

                    def turn_page(p):
                        pe.wait_ge(copied[p % 2], i * 8 + (4 * u + p // 2 + 1))
                        for c in range(WC):
                            m = TR(bank[p % 2][:, c * P:(c + 1) * P], kp[:, p, c * P:(c + 1) * P], ident[:, :])
                        m.then_inc(s("k_page_turned"), 1)

                    MM(bank[2 + u][:, :], row0[:, :], bias2, start=True, stop=False)
                    pe.wait_ge(s(f"k_loaded{u}"), i * 128 + 128)
                    turn_page(0)
                    for p in range(NPAGE):
                        if p + 1 < NPAGE:
                            turn_page(p + 1)
                        pe.wait_ge(copied[p % 2], i * 8 + (4 * u + p // 2 + 2))
                        for c in range(WC):
                            m = MM(bank[2 + u][:, 64 * p + 16 * c:64 * p + 16 * (c + 1)], k_turn[:, p % 2, c * P:(c + 1) * P],
                                   q_pair[:, bass.ds(i * 2 + u, 1), c, :].rearrange("p b k -> p (b k)"),
                                   start=False, stop=p == NPAGE - 1 and c == WC - 1)
                    m.then_inc(s("z_done"), 1)
                for u in range(2):
                    pe.wait_ge(s("soft_ready"), i * 4 + (2 * u + 2))
                    MM(bank[2 + u][:, :], neg_tri[:, :], soft[:, u, :], start=False, stop=False, skip_group_check=True)
                    MM(bank[2 + u][:, :], neg_ones[:, :], later[:, u, :], start=False, stop=True,
                       skip_group_check=True).then_inc(s("c_done"), 1)
                for u in range(2):
                    vp = slot((3, 1)[u], NPAGE, W)
                    pe.wait_ge(s("wgt_ready"), i * 2 + (u + 1))
                    pe.wait_ge(s(f"v_loaded{u}"), i * 128 + 128)
                    pe.wait_ge(s("o_copied"), i * 4 + (2 * u + 2))
                    for c in range(WC):
                        for p in range(NPAGE):
                            MM(bank[5 + u][:, 16 * c:16 * (c + 1)], vp[:, p, c * P:(c + 1) * P],
                               wgt[:, u, 64 * p + 16 * c:64 * p + 16 * (c + 1)], start=p == 0, stop=False)
                        m = MM(bank[5 + u][:, 16 * c:16 * (c + 1)], v_tok[0:TS, 2, c * P:(c + 1) * P],
                               w_new[:, bass.ds(i * 2 + u, 1), 16 * c:16 * (c + 1)].rearrange("p b k -> p (b k)"),
                               start=False, stop=True)
                    m.then_inc(s("o_done"), 1)

            def p_scores(hd):
                z, c = bank[hd % 2], hd // 2
                MM(z[:, 0:SEQ], proj[:, TK + c, 0:P], q_head[:, hd, :], start=True, stop=True)
                MM(z[:, SEQ:3 * P], proj[:, TK + c, P:SEQ], q_head[:, hd, P:SEQ], start=False, stop=True,
                   skip_group_check=True).then_inc(s("z_done"), 1)

            def p_out(hd):
                o_, c, wg = bank[2 + hd % 2], hd // 2, wgt[:, hd % 2, :]
                pe.wait_ge(s("pw_ready"), hd + 1)
                if hd >= 2:
                    pe.wait_ge(s("att_ready"), hd - 1)
                MM(o_[:, 0:SEQ], v_tok[:, 0, c * P:(c + 1) * P], wg[:, 0:SEQ], start=True, stop=False)
                MM(o_[:, P:SEQ], v_tok[:, 1, c * P:(c + 1) * P], wg[:, SEQ:3 * P], start=False, stop=True
                   ).then_inc(s("po_done"), 1)

            pe.wait_ge(s("even_copied"), 33)
            pe.wait_ge(s("odd_copied"), 33)
            p_scores(0)
            for hd in range(H):
                z, sf = bank[hd % 2], soft[:, hd % 2, :]
                if hd >= 1:
                    p_out(hd - 1)
                if hd + 1 < H:
                    p_scores(hd + 1)
                pe.wait_ge(s("p_soft"), hd + 1)
                MM(z[:, 0:3 * P], neg_tri[:, :], sf[:, 0:3 * P], start=False, stop=False, skip_group_check=True)
                MM(z[:, P:SEQ], neg_ones[:, :], sf[:, SEQ:3 * P], start=False, stop=True,
                   skip_group_check=True).then_inc(s("c_done"), 1)
            p_out(H - 1)

            pe.wait_ge(s("o_copied"), 4 + 2 * NB)
            n_, L = 0, 0
            for n in (1, 2, 0):
                src = {0: att, 1: proj[:, TB:TB + WC, :], 2: proj[:, TA:TA + WC, :]}[n]
                if n == 0:
                    pe.wait_ge(s("att_ready"), H)
                loaded(pe, L)
                for m_ in range(DC):
                    if n_ >= 4:
                        pe.wait_ge(s("merged"), n_ - 3)
                    for k in range(WC):
                        m = MM(bank[4 + n_ % 4][:, 0:T], slot(L % 4, WC, D)[:, k, m_ * P:(m_ + 1) * P], src[:, k, :],
                               start=k == 0, stop=k == WC - 1)
                    m.then_inc(s("branch_done"), 1)
                    n_ += 1
                L += 1
            pe.wait_ge(s("merged"), 3 * DC)
            for j in range(2):
                loaded(pe, L)
                for m_ in range(4):
                    if j:
                        pe.wait_ge(s("out_added"), m_ + 1)
                    for k in range(DC):
                        m = MM(bank[m_][:, 0:T], slot(L % 4, DC, GROUP)[:, k, m_ * P:(m_ + 1) * P], merged[:, k, :],
                               start=k == 0, stop=k == DC - 1)
                    m.then_inc(s("out_done"), 1)
                L += 1

            pe.wait_ge(s("norm_squared"), 6)
            norm_sum(3, h, DC)
            pe.wait_ge(s("h_ready"), 2 * DC)
            pe.wait_ge(s("small_loaded"), 9 * 16)
            for i_, (t0, n) in enumerate(BLK):
                for k in range(DC):
                    m = MM(bank[i_][0:n, 0:NG + NE], h[:, k, t0:t0 + n], w_router[:, k, :], start=k == 0, stop=k == DC - 1)
                m.then_inc(s("logits_done"), 1)
            pe.wait_ge(s("h_ready"), 2 * DC)
            for n_, (i_, q) in enumerate([(i_, q) for i_ in range(3) for q in range(2)]):
                t0, n = BLK[i_]
                if n_ >= 4:
                    pe.wait_ge(s("h_tok_ready"), n_ - 3)
                for c in range(4):
                    m = TR(bank[4 + n_ % 4][0:n, c * P:(c + 1) * P], h[:, 4 * q + c, t0:t0 + n], ident[:, :])
                m.then_inc(s("h_tok_turned"), 1)
            pe.wait_ge(s("comb_ready"), 1)
            for i_, (t0, n) in enumerate(BLK):
                m = TR(bank[3][0:NE, t0:t0 + n], R["comb"][0:n, i_, :], ident[0:n, 0:n])
            m.then_inc(s("comb_turned"), 1)
            pe.wait_ge(s("slots_ready"), 1)
            for i_, (t0, n) in enumerate(BLK):
                TR(bank[3][0:n, 16 * i_:16 * i_ + NE], taken[:, t0:t0 + n], ident[0:NE, 0:NE])
            TR(bank[3][0:1, 64:64 + NE], rank[:, T - 1:T], ident[0:NE, 0:NE]).then_inc(s("slots_turned"), 1)
            pe.wait_ge(s("crowded_ready"), 1)
            with pe.If(pe.value_load(crowded[:, :], min_val=0, max_val=1) == 0):
                pe.wait_ge(s("h_tok_ready"), 6)

                def gather(e, u):
                    pe.wait_ge(s("pick_ready"), e)
                    for c in range(DC):
                        for i_ in range(3):
                            m = MM(bank[c // 4][:, (c % 4) * P:(c % 4 + 1) * P], h_tok[:, i_, c * P:(c + 1) * P],
                                   pick_t[:, u, i_, :], start=i_ == 0, stop=i_ == 2)
                        if c == 3:
                            m.then_inc(s("gathered_low"), 1)
                    m.then_inc(s("gathered_high"), 1)

                def scatter(e, u):
                    pe.wait_ge(s("share_ready"), e)
                    pe.wait_ge(s("y_low"), e)
                    pe.wait_ge(s("y_high"), e)
                    for c in range(DC):
                        if c >= 4:
                            pe.wait_ge(s("down_added"), e * 8 + (c - 11))
                        MM(bank[(6, 7, 3, 4)[c % 4]][:, 0:T], y_exp[:, c * P:(c + 1) * P], weigh_s[:, u, :],
                           start=True, stop=True).then_inc(s("spread_done"), 1)

                def turn(i, first, last):
                    for e in range(4):
                        u, n = e % 2, i * 4 + (e + 1)
                        later_ = not (first and e == 0)
                        pe.wait_ge(s("h_exp_low"), n)
                        pe.wait_ge(s("h_exp_high"), n)
                        if not (first and e < 2):
                            pe.wait_ge(s("down_added"), n * 8 + (-16))
                        for r, name in enumerate(("gate_done", "up_done")):
                            loaded(pe, L + 3 * e + r, i, 12)
                            for k in range(DC):
                                m = MM(bank[3 + r][:, :], h_exp[:, u, k * P:(k + 1) * P],
                                       slot((L + 3 * e + r) % 4, DC, DE)[:, k, :], start=k == 0, stop=k == DC - 1)
                            m.then_inc(s(name), 1)
                        pe.wait_ge(s("weigh_ready"), n)
                        for i_ in range(3):
                            m = TR(bank[2][:, i_ * P:(i_ + 1) * P], weigh_t[:, u, i_, :], ident[:, :])
                        m.then_inc(s("weigh_turned"), 1)
                        if not (last and e == 3):
                            gather(n + 1, 1 - u)
                        pe.wait_ge(s("act_ready"), n)
                        for k in range(DE // P):
                            m = TR(bank[5][:, k * P:(k + 1) * P], act_s[:, k * P:(k + 1) * P], ident[:, :])
                        m.then_inc(s("act_turned"), 1)
                        if later_:
                            scatter(n + (-1), 1 - u)
                        loaded(pe, L + 3 * e + 2, i, 12)
                        pe.wait_ge(s("act_f_ready"), n)
                        for q in range(2):
                            if later_:
                                pe.wait_ge(s("down_added"), n * 8 + (q - 11))
                            for k in range(DE // P):
                                m = MM(bank[6 + q][:, :], act_ft[:, k * P:(k + 1) * P],
                                       slot((L + 3 * e + 2) % 4, DE // P, D)[:, k, q * 512:(q + 1) * 512],
                                       start=k == 0, stop=k == DE // P - 1)
                            m.then_inc(s(("down_low", "down_done")[q]), 1)

                gather(1, 0)
                turn(0, True, False)
                with pe.Fori(1, NE // 4 - 1) as i:
                    turn(i, False, False)
                turn(NE // 4 - 1, False, True)
                scatter(NE, 1)
            with pe.Else():
                pe.wait_ge(s("share_row_ready"), 1)
                pe.wait_ge(s("expert_row_ready"), 1)
                for e in range(NE):
                    if e >= 4:
                        pe.wait_ge(s("share_ready"), e - 3)
                    MM(bank[4 + e % 4][:, 0:T], expert_row[:, e, :], share_row, start=True, stop=True
                       ).then_inc(s("spread_done"), 1)
                pe.wait_ge(s("share_ready"), NE)

                with pe.Fori(0, NE // 4) as i:
                    for e in range(4):
                        for r, name in enumerate(("gate", "up")):
                            loaded(pe, L + 3 * e + r, i, 12)
                            for m_ in range(4):
                                if r == 0:
                                    pe.wait_ge(s("down_added"), i * 32 + (8 * e + m_ + 5))
                                for k in range(DC):
                                    m = MM(bank[4 * r + m_][:, 0:T], slot((L + 3 * e + r) % 4, DC, DE)[:, k, m_ * P:(m_ + 1) * P],
                                           h[:, k, :], start=k == 0, stop=k == DC - 1)
                                m.then_inc(s(name + "_done"), 1)
                                loaded(pe, L + 3 * e + 2, i, 12)
                        for m_ in range(DC):
                            if m_ >= 4:
                                pe.wait_ge(s("down_added"), i * 32 + (8 * e + m_ + 5))
                            for k in range(DE // P):
                                if m_ == 0:
                                    pe.wait_ge(s("act_ready"), i * 16 + (4 * e + k + 1))
                                m = MM(bank[m_ % 4][:, 0:T], slot((L + 3 * e + 2) % 4, DE // P, D)[:, k, m_ * P:(m_ + 1) * P],
                                       act_t[:, k, :], start=k == 0, stop=k == DE // P - 1)
                            m.then_inc(s("down_done"), 1)
            L += 3 * NE

            pe.wait_ge(s("p_loaded"), 32)
            pe.wait_ge(s("moe_added"), 1)
            for i_, (t0, n) in enumerate(BLK):
                for c in range(PLE // P):
                    m = TR(bank[4 + c][:, t0:t0 + n], p_tok[0:n, i_, c * P:(c + 1) * P], ident[0:n, 0:n])
            m.then_inc(s("p_turned"), 1)
            pe.wait_ge(s("norm_squared"), 8)
            norm_sum(4, h, DC)
            pe.wait_ge(s("h_ready"), 3 * DC)
            pe.wait_ge(s("p_ready"), 2)
            loaded(pe, L + 2)
            for m_ in range(DC):
                if m_ % 4 == 0:
                    loaded(pe, L + m_ // 4)
                if m_ >= 4:
                    pe.wait_ge(s("pple_added"), m_ - 3)
                for k in range(DC):
                    m = MM(bank[m_ % 4][:, 0:T], slot((L + m_ // 4) % 4, DC, GROUP)[:, k, (m_ % 4) * P:(m_ % 4 + 1) * P],
                           h[:, k, :], start=k == 0, stop=k == DC - 1)
                m.then_inc(s("pg_done"), 1)
                for k in range(PLE // P):
                    m = MM(bank[4 + m_ % 4][:, 0:T], slot((L + 2) % 4, PLE // P, D)[:, k, m_ * P:(m_ + 1) * P],
                           p_feat[:, k, :], start=k == 0, stop=k == PLE // P - 1)
                m.then_inc(s("pp_done"), 1)

            pe.wait_ge(s("norm_squared"), 10)
            norm_sum(5, h, DC)
            pe.wait_ge(s("h_ready"), 4 * DC)
            for i_, (t0, n) in enumerate(BLK):
                for q in range(2):
                    for c in range(4):
                        m = TR(bank[2 * i_ + q][0:n, c * P:(c + 1) * P], h[:, 4 * q + c, t0:t0 + n], ident[:, :])
                    m.then_inc(s("y_turned"), 1)


_INS = ["x_prompt", "x_sample", "p_prompt", "p_sample", "cache_k", "cache_v", "page_table",
        "state_ssm", "state_ssm_conv", "state_cf_conv", "norm_mix", "w_in", "sb_bias",
        "ssm_conv_w", "ssm_conv_b", "dt_bias", "a_log", "d_skip", "ssm_norm",
        "cf_conv_w", "cf_conv_b", "cf_ln_g", "cf_ln_b", "w_branch", "w_out",
        "norm_ffn", "w_router_group", "b_router_group", "w_router_expert", "b_router_expert",
        "w_expert_gate", "w_expert_up", "w_expert_down", "norm_ple", "w_ple_gate", "w_ple_proj",
        "norm_final"]
_OUTS = [("y_prompt", (1, 256, 1024)), ("y_sample", (8, 8, 1024)),
         ("k_prompt", (1, 1, 256, 8, 64)), ("v_prompt", (1, 1, 256, 8, 64)),
         ("ssm_prompt", (1, 1, 8, 64, 128)), ("ssm_conv_prompt", (1, 1, 3, 1024)),
         ("cf_conv_prompt", (1, 1, 30, 512)),
         ("k_sample", (1, 8, 8, 8, 64)), ("v_sample", (1, 8, 8, 8, 64)),
         ("ssm_sample", (1, 8, 8, 64, 128)), ("ssm_conv_sample", (1, 8, 3, 1024)),
         ("cf_conv_sample", (1, 8, 30, 512))]


def kernel(**inputs):
    import numpy as _np
    import concourse.bacc as _bacc
    from concourse import mybir as _mybir
    from concourse.bass_utils import run_bass_kernel_spmd as _run

    nc = _bacc.Bacc("TRN2", target_bir_lowering=False, num_devices=1)
    arrays, ins, outs = {}, {}, {}
    for name in _INS:
        arr = _np.ascontiguousarray(inputs[name])
        arrays[f"in_{name}"] = arr
        ins[name] = nc.dram_tensor(f"in_{name}", arr.shape, _mybir.dt.from_np(arr.dtype), kind="ExternalInput").ap()
    for name, shape in _OUTS:
        outs[name] = nc.dram_tensor(f"out_{name}", shape, _mybir.dt.float32, kind="ExternalOutput").ap()
    build(nc, ins, outs)
    r = _run(nc, [arrays], core_ids=[0])
    return tuple(r.results[0][f"out_{name}"] for name, _ in _OUTS)
```
